# Optimizing a Trainium2 kernel written in Bass

```python
import jax, jax.numpy as jnp
from jax import lax
import numpy as np
import math

D_MODEL = 1024
BATCH = 1
SEQ = 512
DEPTH = 1

POOL_WIDTH = D_MODEL // 2
POOL_GROUPS = 4
POOL_GROUP_WIDTH = POOL_WIDTH // POOL_GROUPS
POOL_WINDOWS = (2, 4, 8, 16)
CONV_WIDTH = D_MODEL // 2
CONV_KERNEL = 31
N_BRANCHES = 2
IN_WIDTH = POOL_WIDTH + 2 * CONV_WIDTH + N_BRANCHES * D_MODEL
PEER_HEADS = 8
PEER_KEY_DIM = 256
PEER_HALF_DIM = PEER_KEY_DIM // 2
N_KEYS = 128
N_EXPERTS = N_KEYS * N_KEYS
PEER_TOPK_HALF = 16
PEER_TOPK = 16
PEER_CHUNK = 128
N_MOD = 6
EPS = 1e-6


def rmsnorm(x, g):
    xf = x.astype(jnp.float32)
    y = xf * lax.rsqrt(jnp.mean(xf * xf, axis=-1, keepdims=True) + EPS)
    return (y * g.astype(jnp.float32)).astype(x.dtype)

def layernorm(x, g, b):
    xf = x.astype(jnp.float32)
    mu = jnp.mean(xf, axis=-1, keepdims=True)
    var = jnp.mean(jnp.square(xf - mu), axis=-1, keepdims=True)
    y = (xf - mu) * lax.rsqrt(var + EPS)
    return (y * g.astype(jnp.float32) + b.astype(jnp.float32)).astype(x.dtype)

def causal_window_mean(xg, w):
    s = xg.shape[1]
    xf = xg.astype(jnp.float32)
    cs = jnp.cumsum(xf, axis=1)
    shifted = jnp.pad(cs, ((0, 0), (w, 0), (0, 0)))[:, :s]
    count = jnp.minimum(jnp.arange(1, s + 1), w).astype(jnp.float32)[None, :, None]
    return ((cs - shifted) / count).astype(xg.dtype)

def pool_branch(p, pool_w, pool_scale, pool_up):
    b, s, _ = p.shape
    pooled = jnp.concatenate(
        [causal_window_mean(p[..., i * POOL_GROUP_WIDTH:(i + 1) * POOL_GROUP_WIDTH], w)
         for i, w in enumerate(POOL_WINDOWS)], axis=-1)
    mixed = (pooled - p).reshape(b, s, POOL_GROUPS, POOL_GROUP_WIDTH)
    mixed = jnp.einsum('bsgc,gcd->bsgd', mixed, pool_w).reshape(b, s, POOL_WIDTH)
    return (mixed * pool_scale) @ pool_up

def conformer_branch(a, dw_kernel, dw_bias, ln_g, ln_b, conv_out):
    glu = a[..., :CONV_WIDTH] * jax.nn.sigmoid(a[..., CONV_WIDTH:])
    y = lax.conv_general_dilated(
        glu, dw_kernel[:, None, :].astype(glu.dtype), window_strides=(1,),
        padding=[(CONV_KERNEL - 1, 0)], dimension_numbers=('NWC', 'WIO', 'NWC'),
        feature_group_count=CONV_WIDTH) + dw_bias
    y = layernorm(y, ln_g, ln_b)
    y = y * jax.nn.sigmoid(y)
    return y @ conv_out

def peer(h, w_query, keys_1, keys_2, expert_u, expert_v):
    b, s, d = h.shape
    flat = h.reshape(b * s // PEER_CHUNK, PEER_CHUNK, d)

    def chunk_fn(hc):
        q = (hc @ w_query).reshape(PEER_CHUNK, PEER_HEADS, PEER_KEY_DIM)
        s1 = jnp.einsum('chk,nk->chn', q[..., :PEER_HALF_DIM], keys_1)
        s2 = jnp.einsum('chk,nk->chn', q[..., PEER_HALF_DIM:], keys_2)
        v1, i1 = lax.top_k(s1, PEER_TOPK_HALF)
        v2, i2 = lax.top_k(s2, PEER_TOPK_HALF)
        cand = (v1[..., :, None] + v2[..., None, :]).reshape(PEER_CHUNK, PEER_HEADS, -1)
        cand_idx = (i1[..., :, None] * N_KEYS + i2[..., None, :]).reshape(PEER_CHUNK, PEER_HEADS, -1)
        top_s, pos = lax.top_k(cand, PEER_TOPK)
        experts = jnp.take_along_axis(cand_idx, pos, axis=-1)
        gate = jax.nn.softmax(top_s.astype(jnp.float32), axis=-1).astype(hc.dtype)
        u = jnp.take(expert_u, experts, axis=0)
        act = jax.nn.gelu(jnp.einsum('chkd,cd->chk', u, hc))
        v = jnp.take(expert_v, experts, axis=0)
        return jnp.einsum('chk,chkd->cd', gate * act, v)

    return lax.map(chunk_fn, flat).reshape(b, s, d)

def first_inputs(seed: int = 0) -> dict:
    key = jax.random.key(seed)
    ks = jax.random.split(key, 24)

    def nrm(k, shape, scale):
        return jax.random.normal(k, shape, jnp.float32) * scale

    def gain(k, shape):
        return 1.0 + 0.05 * jax.random.normal(k, shape, jnp.float32)

    L = DEPTH
    return {
        "x": nrm(ks[0], (BATCH, SEQ, D_MODEL), 1.0),
        "c": nrm(ks[1], (BATCH, D_MODEL), 1.0),
        "ada_w": nrm(ks[2], (L, D_MODEL, N_MOD * D_MODEL), 0.5 * D_MODEL ** -0.5),
        "ada_b": nrm(ks[3], (L, N_MOD * D_MODEL), 0.01),
        "norm1_g": gain(ks[4], (L, D_MODEL)),
        "w_in": nrm(ks[5], (L, D_MODEL, IN_WIDTH), D_MODEL ** -0.5),
        "b_in": nrm(ks[6], (L, IN_WIDTH), 0.01),
        "pool_w": nrm(ks[7], (L, POOL_GROUPS, POOL_GROUP_WIDTH, POOL_GROUP_WIDTH), POOL_GROUP_WIDTH ** -0.5),
        "pool_scale": gain(ks[8], (L, POOL_WIDTH)),
        "pool_up": nrm(ks[9], (L, POOL_WIDTH, D_MODEL), POOL_WIDTH ** -0.5),
        "dw_kernel": nrm(ks[10], (L, CONV_KERNEL, CONV_WIDTH), CONV_KERNEL ** -0.5),
        "dw_bias": nrm(ks[11], (L, CONV_WIDTH), 0.01),
        "conv_ln_g": gain(ks[12], (L, CONV_WIDTH)),
        "conv_ln_b": nrm(ks[13], (L, CONV_WIDTH), 0.01),
        "conv_out": nrm(ks[14], (L, CONV_WIDTH, D_MODEL), CONV_WIDTH ** -0.5),
        "w_out": nrm(ks[15], (L, D_MODEL, D_MODEL), D_MODEL ** -0.5),
        "norm2_g": gain(ks[16], (L, D_MODEL)),
        "w_query": nrm(ks[17], (L, D_MODEL, PEER_HEADS * PEER_KEY_DIM), D_MODEL ** -0.5),
        "sub_keys_1": nrm(ks[18], (L, N_KEYS, PEER_HALF_DIM), PEER_HALF_DIM ** -0.5),
        "sub_keys_2": nrm(ks[19], (L, N_KEYS, PEER_HALF_DIM), PEER_HALF_DIM ** -0.5),
        "expert_u": nrm(ks[20], (L, N_EXPERTS, D_MODEL), D_MODEL ** -0.5),
        "expert_v": nrm(ks[21], (L, N_EXPERTS, D_MODEL), PEER_HEADS ** -0.5),
        "final_g": gain(ks[22], (D_MODEL,)),
    }

def first_block(x, c, ada_w, ada_b, norm1_g, w_in, b_in, pool_w, pool_scale, pool_up,
              dw_kernel, dw_bias, conv_ln_g, conv_ln_b, conv_out, w_out, norm2_g,
              w_query, sub_keys_1, sub_keys_2, expert_u, expert_v, final_g):
    c_act = jax.nn.silu(c)
    for l in range(DEPTH):
        mod = c_act @ ada_w[l] + ada_b[l]
        shift1, scale1, gate1, shift2, scale2, gate2 = [
            m[:, None, :] for m in jnp.split(mod, N_MOD, axis=-1)]

        h = rmsnorm(x, norm1_g[l]) * (1.0 + scale1) + shift1
        proj = h @ w_in[l] + b_in[l]
        p = proj[..., :POOL_WIDTH]
        a = proj[..., POOL_WIDTH:POOL_WIDTH + 2 * CONV_WIDTH]
        g = proj[..., POOL_WIDTH + 2 * CONV_WIDTH:]
        y_pool = pool_branch(p, pool_w[l], pool_scale[l], pool_up[l])
        y_conv = conformer_branch(a, dw_kernel[l], dw_bias[l], conv_ln_g[l], conv_ln_b[l], conv_out[l])
        merged = jax.nn.sigmoid(g[..., :D_MODEL]) * y_pool + jax.nn.sigmoid(g[..., D_MODEL:]) * y_conv
        x = x + gate1 * (merged @ w_out[l])

        h2 = rmsnorm(x, norm2_g[l]) * (1.0 + scale2) + shift2
        x = x + gate2 * peer(h2, w_query[l], sub_keys_1[l], sub_keys_2[l], expert_u[l], expert_v[l])
    return rmsnorm(x, final_g)


HEAD_DIM = 64
N_DIFF_HEADS = (D_MODEL // 2) // (2 * HEAD_DIM)
N_DIL_HEADS = (D_MODEL // 2) // HEAD_DIM
DIFF_WIDTH = N_DIFF_HEADS * 2 * HEAD_DIM
DIL_WIDTH = N_DIL_HEADS * HEAD_DIM
MIX_WIDTH = DIFF_WIDTH + DIL_WIDTH
D_FF = 256 * ((8 * D_MODEL // 3 + 255) // 256)
DILATED_CONFIGS = ((128, 1), (512, 4), (2048, 16))
NUM_BUCKETS = 32
MAX_DISTANCE = 2048
N_BIAS_COLS = 2 * N_DIFF_HEADS + N_DIL_HEADS
Q_BLOCK = 128


def rmsnorm_2(x, g):
    x32 = x.astype(jnp.float32)
    y = x32 * lax.rsqrt(jnp.mean(x32 * x32, axis=-1, keepdims=True) + EPS)
    return (y * g.astype(jnp.float32)).astype(x.dtype)

def swiglu(x, w_gate, w_up, w_down):
    return (jax.nn.silu(x @ w_gate) * (x @ w_up)) @ w_down

def t5_bucket(dist):
    n = jnp.maximum(dist, 0)
    max_exact = NUM_BUCKETS // 2
    nf = jnp.maximum(n, 1).astype(jnp.float32)
    large = max_exact + (jnp.log(nf / max_exact) / math.log(MAX_DISTANCE / max_exact)
                         * (NUM_BUCKETS - max_exact)).astype(jnp.int32)
    large = jnp.minimum(large, NUM_BUCKETS - 1)
    return jnp.where(n < max_exact, n, large)

def lambda_init(layer):
    return 0.8 - 0.6 * math.exp(-0.3 * layer)

def diff_attention(q, k, v, lam, bias_table):
    B, H, _, S, Dh = q.shape
    nb = S // Q_BLOCK
    scale = Dh ** -0.5
    k_pos = jnp.arange(S)
    q_blocks = q.reshape(B, H, 2, nb, Q_BLOCK, Dh).transpose(3, 0, 1, 2, 4, 5)
    v32 = v.astype(jnp.float32)
    table = bias_table.astype(jnp.float32)

    def one_block(args):
        q_blk, start = args
        s = jnp.einsum('bhmqd,bhmkd->bhmqk', q_blk, k).astype(jnp.float32) * scale
        dist = (start + jnp.arange(Q_BLOCK))[:, None] - k_pos[None, :]
        bias = table[t5_bucket(dist)].transpose(2, 0, 1).reshape(H, 2, Q_BLOCK, S)
        s = jnp.where(dist >= 0, s + bias, -jnp.inf)
        p = jax.nn.softmax(s, axis=-1)
        a = p[:, :, 0] - lam * p[:, :, 1]
        return jnp.einsum('bhqk,bhkd->bhqd', a, v32)

    out = lax.map(one_block, (q_blocks, jnp.arange(nb) * Q_BLOCK))
    return out.transpose(1, 2, 0, 3, 4).reshape(B, H, S, 2 * Dh)

def dilated_branch(q, k, v, window, dil, bias_table):
    B, H, S, Dh = q.shape
    W = window // dil
    Ld = S // dil
    nb = -(-Ld // W)
    Lp = nb * W
    scale = Dh ** -0.5

    def regroup(t):
        t = t.reshape(B, H, Ld, dil, Dh).transpose(0, 1, 3, 2, 4)
        t = jnp.pad(t, ((0, 0), (0, 0), (0, 0), (0, Lp - Ld), (0, 0)))
        return t.reshape(B, H, dil, nb, W, Dh)

    def with_prev(t):
        prev = jnp.pad(t, ((0, 0), (0, 0), (0, 0), (1, 0), (0, 0), (0, 0)))[:, :, :, :nb]
        return jnp.concatenate([prev, t], axis=4)

    qg = regroup(q)
    kw = with_prev(regroup(k))
    vw = with_prev(regroup(v))
    s = jnp.einsum('bhrnqd,bhrnkd->bhrnqk', qg, kw).astype(jnp.float32) * scale
    a_idx = jnp.arange(W)[:, None]
    c_idx = jnp.arange(2 * W)[None, :]
    dist = a_idx + W - c_idx
    key_idx = jnp.arange(nb)[:, None, None] * W - W + c_idx[None]
    valid = ((dist >= 0) & (dist <= W))[None] & (key_idx >= 0)
    bias = bias_table.astype(jnp.float32)[t5_bucket(dist * dil)].transpose(2, 0, 1)
    s = jnp.where(valid, s + bias[None, :, None, None], -jnp.inf)
    m = jnp.max(s, axis=-1)
    e = jnp.exp(s - m[..., None])
    l = jnp.sum(e, axis=-1)
    o = jnp.einsum('bhrnqk,bhrnkd->bhrnqd', e, vw.astype(jnp.float32)) / l[..., None]

    def restore(t):
        tail = t.shape[5:]
        t = t.reshape((B, H, dil, Lp) + tail)[:, :, :, :Ld]
        t = jnp.moveaxis(t, 2, 3)
        return t.reshape((B, H, S) + tail)

    return restore(o), restore(m), restore(l)

def dilated_attention(q, k, v, bias_table):
    outs = [dilated_branch(q, k, v, w, d, bias_table) for (w, d) in DILATED_CONFIGS]
    m_all = jnp.stack([br[1] for br in outs])
    l_all = jnp.stack([br[2] for br in outs])
    o_all = jnp.stack([br[0] for br in outs])
    wts = l_all * jnp.exp(m_all - jnp.max(m_all, axis=0, keepdims=True))
    wts = wts / jnp.sum(wts, axis=0, keepdims=True)
    return jnp.sum(wts[..., None] * o_all, axis=0)

def token_mixer(h, w_in, w_out, lq1, lk1, lq2, lk2, subln_gain, rel_bias, layer):
    B, S, _ = h.shape
    proj = h @ w_in
    qa, ka, va, qb, kb, vb = jnp.split(
        proj, [DIFF_WIDTH, 2 * DIFF_WIDTH, 3 * DIFF_WIDTH,
               3 * DIFF_WIDTH + DIL_WIDTH, 3 * DIFF_WIDTH + 2 * DIL_WIDTH], axis=-1)
    qa = qa.reshape(B, S, N_DIFF_HEADS, 2, HEAD_DIM).transpose(0, 2, 3, 1, 4)
    ka = ka.reshape(B, S, N_DIFF_HEADS, 2, HEAD_DIM).transpose(0, 2, 3, 1, 4)
    va = va.reshape(B, S, N_DIFF_HEADS, 2 * HEAD_DIM).transpose(0, 2, 1, 3)
    lam0 = lambda_init(layer)
    f32 = jnp.float32
    lam = (jnp.exp(jnp.sum(lq1.astype(f32) * lk1.astype(f32)))
           - jnp.exp(jnp.sum(lq2.astype(f32) * lk2.astype(f32))) + lam0)
    oa = diff_attention(qa, ka, va, lam, rel_bias[:, :2 * N_DIFF_HEADS])
    oa = rmsnorm_2(oa, subln_gain) * (1.0 - lam0)
    oa = oa.transpose(0, 2, 1, 3).reshape(B, S, DIFF_WIDTH)
    qb = qb.reshape(B, S, N_DIL_HEADS, HEAD_DIM).transpose(0, 2, 1, 3)
    kb = kb.reshape(B, S, N_DIL_HEADS, HEAD_DIM).transpose(0, 2, 1, 3)
    vb = vb.reshape(B, S, N_DIL_HEADS, HEAD_DIM).transpose(0, 2, 1, 3)
    ob = dilated_attention(qb, kb, vb, rel_bias[:, 2 * N_DIFF_HEADS:])
    ob = ob.transpose(0, 2, 1, 3).reshape(B, S, DIL_WIDTH)
    mixed = jnp.concatenate([oa, ob], axis=-1).astype(h.dtype)
    return mixed @ w_out

def second_inputs(seed: int = 0) -> dict:
    key = jax.random.key(seed)
    ks = jax.random.split(key, 20)
    f32 = jnp.float32
    nrm = lambda k, shape, scale: jax.random.normal(k, shape, f32) * scale
    gain = lambda k, shape: 1.0 + 0.05 * jax.random.normal(k, shape, f32)
    return {
        'x': jax.random.normal(ks[0], (BATCH, SEQ, D_MODEL), f32),
        'ffn1_norm': gain(ks[1], (DEPTH, D_MODEL)),
        'ffn1_w_gate': nrm(ks[2], (DEPTH, D_MODEL, D_FF), D_MODEL ** -0.5),
        'ffn1_w_up': nrm(ks[3], (DEPTH, D_MODEL, D_FF), D_MODEL ** -0.5),
        'ffn1_w_down': nrm(ks[4], (DEPTH, D_FF, D_MODEL), D_FF ** -0.5),
        'mix_norm': gain(ks[5], (DEPTH, D_MODEL)),
        'w_in': nrm(ks[6], (DEPTH, D_MODEL, 3 * MIX_WIDTH), D_MODEL ** -0.5),
        'lambda_q1': nrm(ks[7], (DEPTH, HEAD_DIM), 0.1),
        'lambda_k1': nrm(ks[8], (DEPTH, HEAD_DIM), 0.1),
        'lambda_q2': nrm(ks[9], (DEPTH, HEAD_DIM), 0.1),
        'lambda_k2': nrm(ks[10], (DEPTH, HEAD_DIM), 0.1),
        'subln_gain': gain(ks[11], (DEPTH, 2 * HEAD_DIM)),
        'w_out': nrm(ks[12], (DEPTH, MIX_WIDTH, D_MODEL), MIX_WIDTH ** -0.5),
        'ffn2_norm': gain(ks[13], (DEPTH, D_MODEL)),
        'ffn2_w_gate': nrm(ks[14], (DEPTH, D_MODEL, D_FF), D_MODEL ** -0.5),
        'ffn2_w_up': nrm(ks[15], (DEPTH, D_MODEL, D_FF), D_MODEL ** -0.5),
        'ffn2_w_down': nrm(ks[16], (DEPTH, D_FF, D_MODEL), D_FF ** -0.5),
        'rel_bias': nrm(ks[17], (NUM_BUCKETS, N_BIAS_COLS), 0.3),
        'final_norm': gain(ks[18], (D_MODEL,)),
    }

def second_block(x, ffn1_norm, ffn1_w_gate, ffn1_w_up, ffn1_w_down, mix_norm, w_in,
              lambda_q1, lambda_k1, lambda_q2, lambda_k2, subln_gain, w_out,
              ffn2_norm, ffn2_w_gate, ffn2_w_up, ffn2_w_down, rel_bias, final_norm):
    for layer in range(DEPTH):
        x = x + 0.5 * swiglu(rmsnorm_2(x, ffn1_norm[layer]),
                             ffn1_w_gate[layer], ffn1_w_up[layer], ffn1_w_down[layer])
        x = x + token_mixer(rmsnorm_2(x, mix_norm[layer]), w_in[layer], w_out[layer],
                            lambda_q1[layer], lambda_k1[layer], lambda_q2[layer], lambda_k2[layer],
                            subln_gain[layer], rel_bias, layer)
        x = x + 0.5 * swiglu(rmsnorm_2(x, ffn2_norm[layer]),
                             ffn2_w_gate[layer], ffn2_w_up[layer], ffn2_w_down[layer])
    return rmsnorm_2(x, final_norm)


def setup_inputs(seed=0):
    out = dict(first_inputs(seed))
    for name, value in second_inputs(seed + 1).items():
        if name != "x":
            out[name + "_2"] = value
    return out


def reference(
    x, c, ada_w, ada_b, norm1_g, w_in, b_in, pool_w, pool_scale, pool_up, dw_kernel, dw_bias,
    conv_ln_g, conv_ln_b, conv_out, w_out, norm2_g, w_query, sub_keys_1, sub_keys_2, expert_u,
    expert_v, final_g, ffn1_norm_2, ffn1_w_gate_2, ffn1_w_up_2, ffn1_w_down_2, mix_norm_2,
    w_in_2, lambda_q1_2, lambda_k1_2, lambda_q2_2, lambda_k2_2, subln_gain_2, w_out_2,
    ffn2_norm_2, ffn2_w_gate_2, ffn2_w_up_2, ffn2_w_down_2, rel_bias_2, final_norm_2,
):
    x = first_block(
        x, c, ada_w, ada_b, norm1_g, w_in, b_in, pool_w, pool_scale, pool_up, dw_kernel,
        dw_bias, conv_ln_g, conv_ln_b, conv_out, w_out, norm2_g, w_query, sub_keys_1,
        sub_keys_2, expert_u, expert_v, final_g,
    )
    return second_block(
        x, ffn1_norm_2, ffn1_w_gate_2, ffn1_w_up_2, ffn1_w_down_2, mix_norm_2, w_in_2,
        lambda_q1_2, lambda_k1_2, lambda_q2_2, lambda_k2_2, subln_gain_2, w_out_2, ffn2_norm_2,
        ffn2_w_gate_2, ffn2_w_up_2, ffn2_w_down_2, rel_bias_2, final_norm_2,
    )


_drawn_inputs = setup_inputs


def setup_inputs(seed=0):
    import zlib

    import numpy as np

    out = dict(_drawn_inputs(seed))
    spreads = {}
    factors = {'ada_b': 4.127,
     'norm1_g': 4.018,
     'b_in': 8.0,
     'pool_scale': 5.26,
     'dw_bias': 21.537,
     'conv_ln_g': 13.855,
     'conv_ln_b': 60.373,
     'norm2_g': 10.03,
     'lambda_q1_2': 2.762,
     'lambda_k2_2': 7.878,
     'ffn2_norm_2': 3.183}
    for name, (base, spread) in spreads.items():
        noise = np.random.default_rng([zlib.crc32(name.encode()), seed]).standard_normal(out[name].shape)
        drawn = base * np.exp(spread * noise) if base else spread * noise
        out[name] = __import__('jax').numpy.asarray(drawn.astype(out[name].dtype))
    for name, factor in factors.items():
        out[name] = (out[name] * factor).astype(out[name].dtype)
    return out
```

```python
import math
from collections import deque
from contextlib import ExitStack

import numpy as np

import concourse.bass as bass
from concourse import mybir

F32 = mybir.dt.float32
F32R = mybir.dt.float32r
U32 = mybir.dt.uint32
ALU = mybir.AluOpType
ACT = mybir.ActivationFunctionType
AX_X = mybir.AxisListType.X

P = 128
S = 512
D = 1024
KT = D // P
TT = S // P
POOL_WINDOWS = (2, 4, 8, 16)
PAD_POOL = 16
CONV_K = 31
PAD_CONV = CONV_K - 1
CW = 512
CT = CW // P
HEADS = 8
TOPK = 16
N_KEYS = 128
EXPERT_TILES = N_KEYS
GROUP = 8
N_GROUPS = EXPERT_TILES // GROUP
D_FF = 256 * ((8 * D // 3 + 255) // 256)
FT = D_FF // P
DH = 64
DIFF_HEADS = 4
DIL_HEADS = 8
N_MAPS = 2 * DIFF_HEADS + DIL_HEADS
LAM0 = 0.8 - 0.6 * math.exp(-0.3 * 0)
EPS = 1e-6
NEG = -1.0e30
BIAS_L = 640
SLAB = 8
RAW_SLOTS = 6
SPLIT_SLOTS = 4
SPLIT_AHEAD = 2
GELU_SLOTS = 8
G_SLOTS = 4
CHUNK = 64
TOK4 = 4

COLS = {}
_n = 0
for _name, _w in (("c", 8), ("ada_b", 48), ("norm1_g", 8), ("b_in", 28), ("pool_scale", 4), ("dw_bias", 4),
                  ("conv_ln_g", 4), ("conv_ln_b", 4), ("norm2_g", 8), ("final_g", 8), ("ffn1_norm_2", 8),
                  ("mix_norm_2", 8), ("ffn2_norm_2", 8), ("final_norm_2", 8), ("subln_gain_2", 1),
                  ("dw_kernel", CT * CONV_K)):
    COLS[_name] = (_n, _w)
    _n += _w
N_COLS = _n


class Queue:

    def __init__(self, engine, sem):
        self.engine, self.sem, self.count, self.waited = engine, sem, 0, {}

    def put(self, make, *after, counted=True):
        self.wait(*after)
        instruction = make(self.engine)
        if counted:
            self.count += 1
            instruction.then_inc(self.sem, 1)
        return (self, self.count)

    def wait(self, *after):
        for token in after:
            if token is None:
                continue
            if isinstance(token, list):
                self.wait(*token)
                continue
            source, value = token
            if value > self.waited.get(source, 0):
                self.waited[source] = value
                self.engine.wait_ge(source.sem, value)

    def dma(self, dst, src, counter, *after):
        self.wait(*after)
        counter.count += 16
        self.engine.dma_start(dst, src).then_inc(counter.sem, 16)
        return (counter, counter.count)


class Counter:

    def __init__(self, sem):
        self.sem, self.count = sem, 0


def build(nc, t):
    ctx = ExitStack()
    with ctx:
        program(nc, t, ctx)


def program(nc, t, ctx):
    def sb(name, shape, dt=F32, stack=ctx):
        return stack.enter_context(nc.sbuf_tensor(name, shape, dt))

    def sem(name):
        return ctx.enter_context(nc.semaphore(name))

    def counter(name):
        return Counter(sem(name))

    pe = Queue(nc.tensor, sem("pe_done"))
    act = Queue(nc.scalar, sem("act_done"))
    dve = Queue(nc.vector, sem("dve_done"))
    pool = Queue(nc.gpsimd, sem("pool_done"))
    sp = Queue(nc.sync, sem("sp_done"))

    banks = [ctx.enter_context(nc.psum_tensor(f"bank{i}", [P, S], F32)) for i in range(8)]
    free_banks = deque((b, None) for b in banks)

    def take():
        return free_banks.popleft()

    def give(bank, reader):
        free_banks.append((bank, reader))

    ident = sb("ident", [P, P])
    ones = sb("ones", [P, P])
    iota128 = sb("iota128", [P, P])
    iota16 = sb("iota16", [P, TOPK])
    cols = sb("cols", [P, N_COLS])
    window_fix = sb("window_fix", [P, CT, PAD_POOL])
    mod = sb("mod", [P, 48])
    c_act = sb("c_act", [P, KT])
    gain1 = sb("gain1", [P, KT])
    gain2 = sb("gain2", [P, KT])
    subln = sb("subln", [P, 1])

    def col(name, k, w=1):
        base, width = COLS[name]
        assert k + w <= width
        return cols[:, base + k:base + k + w]

    def modc(part, k, w=1):
        return mod[:, part * KT + k:part * KT + k + w]

    x = sb("x", [P, KT, S])
    h_hi = sb("h_hi", [P, KT, S], F32R)
    h_lo = sb("h_lo", [P, KT, S], F32R)
    tmp = sb("tmp", [P, 4, S])
    rstd = sb("rstd", [P, S])
    raw = sb("raw", [P, RAW_SLOTS, SLAB * P])
    w_hi = sb("w_hi", [P, SPLIT_SLOTS, SLAB * P], F32R)
    w_lo = sb("w_lo", [P, SPLIT_SLOTS, SLAB * P], F32R)

    const_in = counter("const_in")
    x_in = counter("x_in")

    for dst, name in ((cols, "cols"), (ident, "ident"), (ones, "ones"), (window_fix, "window_fix"),
                      (iota128, "iota128"), (iota16, "iota16")):
        consts_ready = act.dma(dst[:], t[name], const_in)
    x_ready = act.dma(x[:], t["x"], x_in)

    tmp_reader = [None] * 4
    tmp_turn = [0]

    def scratch():
        i = tmp_turn[0] % 4
        tmp_turn[0] += 1
        return i, tmp[:, i, :], tmp_reader[i]

    background = []

    def run_background():
        for entry in list(background):
            for _ in range(entry[1]):
                if next(entry[0], "end") == "end":
                    background.remove(entry)
                    break

    def finish(generator):
        for entry in list(background):
            if entry[0] is generator:
                background.remove(entry)
        for _ in generator:
            pass

    order = []

    def plan(name, split=True, slabs=None):
        n = t[name].shape[0]
        order.extend((t[name][i], split) for i in (range(n) if slabs is None else slabs))

    plan("ada_w", split=False, slabs=range(16))
    ada_rest = list(range(16, 48))
    for i in range(t["w_in"].shape[0]):
        plan("w_in", slabs=[i])
        if i < 28:
            plan("ada_w", split=False, slabs=[ada_rest.pop(0)])
    plan("ada_w", split=False, slabs=ada_rest)
    plan("w_merge")
    plan("w_out")
    plan("w_query")
    u_next = GELU_SLOTS
    plan("expert_u", slabs=range(GELU_SLOTS))
    for g in range(N_GROUPS):
        plan("expert_v", slabs=range(g * KT, (g + 1) * KT))
        for _ in range(GROUP):
            if u_next < EXPERT_TILES:
                plan("expert_u", slabs=[u_next])
                u_next += 1
    plan("ffn1_gate_up")
    plan("ffn1_down")
    plan("w_in_2")
    plan("w_out_2")
    plan("ffn2_gate_up")
    plan("ffn2_down")

    raw_in = [counter(f"raw_in{i}") for i in range(RAW_SLOTS)]
    split_reader = [None] * SPLIT_SLOTS
    landed, parts_ready, split_slot = {}, {}, {}
    raw_done = {}
    n_prepared, n_split, used = [0], [0], [0]

    def load():
        i = len(landed)
        while i < len(order) and (i < RAW_SLOTS or i - RAW_SLOTS in raw_done):
            landed[i] = sp.dma(raw[:, i % RAW_SLOTS, :], order[i][0], raw_in[i % RAW_SLOTS], raw_done.get(i - RAW_SLOTS))
            i += 1

    def prepare(i):
        if not order[i][1]:
            return
        k = n_split[0] % SPLIT_SLOTS
        n_split[0] += 1
        split_slot[i] = k
        hi, lo, r = w_hi[:, k, :], w_lo[:, k, :], raw[:, i % RAW_SLOTS, :]
        hi_done = act.put(lambda e: e.copy(hi, r), landed[i], split_reader[k])
        raw_done[i] = parts_ready[i] = dve.put(lambda e: e.tensor_tensor(lo, r, hi.bitcast(F32), ALU.subtract),
                                               landed[i], hi_done)
        load()

    load()

    def open_slab():
        run_background()
        i = used[0]
        while n_prepared[0] <= min(i + SPLIT_AHEAD, len(order) - 1) and n_prepared[0] in landed:
            prepare(n_prepared[0])
            n_prepared[0] += 1
        used[0] += 1
        return i

    def slab_parts(i):
        if order[i][1]:
            return w_hi[:, split_slot[i], :], w_lo[:, split_slot[i], :], parts_ready[i]
        return raw[:, i % RAW_SLOTS, :], None, landed[i]

    def close_slab(i, last):
        if order[i][1]:
            split_reader[split_slot[i]] = last
        else:
            raw_done[i] = last
            load()

    def three(out, a_hi, a_lo, b_hi, b_lo, start, stop, *after):
        pe.put(lambda e: e.matmul(out, a_hi, b_hi, start=start, stop=False), *after, counted=False)
        pe.put(lambda e: e.matmul(out, a_hi, b_lo, start=False, stop=False), counted=False)
        return pe.put(lambda e: e.matmul(out, a_lo, b_hi, start=False, stop=stop))

    cursor = {"slab": None, "block": SLAB}

    def next_block(width=1):
        if cursor["block"] >= SLAB:
            cursor["slab"], cursor["block"] = open_slab(), 0
        i, b = cursor["slab"], cursor["block"]
        cursor["block"] += width
        hi, lo, token = slab_parts(i)
        cut = slice(b * P, (b + width) * P)
        return i, hi[:, cut], None if lo is None else lo[:, cut], token, cursor["block"] >= SLAB

    def project(x_hi, x_lo, kts, after, n=S):
        bank, reader = take()
        for j, k in enumerate(kts):
            i, hi, lo, token, last = next_block()
            done = three(bank[:, 0:n], hi, lo, x_hi[:, k, :], x_lo[:, k, :], j == 0, j == len(kts) - 1,
                         token, reader if j == 0 else None, after)
            if last:
                close_slab(i, done)
        return bank, done

    def split(src, hi, lo, *after):
        a = act.put(lambda e: e.copy(hi, src), *after)
        return dve.put(lambda e: e.tensor_tensor(lo, src, hi.bitcast(F32), ALU.subtract), a, *after)

    def feature_sum(tiles, token, square=True):
        bank, reader = take()
        for j, tile in enumerate(tiles):
            if square:
                i, sq, r = scratch()
                a = act.put(lambda e, sq=sq, tile=tile: e.activation(sq, tile, ACT.Square), token, r)
                done = pe.put(lambda e, sq=sq, j=j: e.matmul(bank[:], ones[:], sq, start=j == 0, stop=j == len(tiles) - 1),
                              a, reader, consts_ready)
                tmp_reader[i] = done
            else:
                done = pe.put(lambda e, tile=tile, j=j: e.matmul(bank[:], ones[:], tile, start=j == 0, stop=j == len(tiles) - 1),
                              token, reader, consts_ready)
        return bank, done

    rstd_reader = [None]

    def inverse_root(bank, token, width):
        a = dve.put(lambda e: e.tensor_scalar(rstd[:], bank[:], 1.0 / width, EPS, ALU.mult, ALU.add), token, rstd_reader[0])
        give(bank, a)
        b = act.put(lambda e: e.activation(rstd[:], rstd[:], ACT.Sqrt), a)
        return dve.put(lambda e: e.reciprocal(rstd[:], rstd[:]), b)

    def normed(gain, shift, x_token, h_reader):
        bank, token = feature_sum([x[:, k, :] for k in range(KT)], x_token)
        r = inverse_root(bank, token, D)
        for k in range(KT):
            i, s, reader = scratch()
            a = dve.put(lambda e, k=k, s=s: e.scalar_tensor_tensor(s, x[:, k, :], gain(k), rstd[:], ALU.mult, ALU.mult),
                        r, reader, x_token)
            hi, lo = h_hi[:, k, :], h_lo[:, k, :]
            if shift is None:
                done = split(s, hi, lo, a, h_reader)
            else:
                b = act.put(lambda e, k=k, s=s, hi=hi: e.activation(hi, s, ACT.Identity, bias=shift(k)), a, h_reader)
                done = dve.put(lambda e, k=k, s=s, hi=hi, lo=lo: e.scalar_tensor_tensor(
                    lo, s, shift(k), hi.bitcast(F32), ALU.add, ALU.subtract), b)
            tmp_reader[i] = done
        rstd_reader[0] = done
        return done

    c_ready = act.put(lambda e: e.activation(c_act[:], col("c", 0, 8), ACT.Silu), consts_ready)

    ada = {"n": 0, "bank": None, "reader": None, "token": {}}

    def ada_column():
        n = ada["n"]
        j = n % KT
        if j == 0:
            ada["bank"], ada["reader"] = take()
        bank = ada["bank"]
        for k in range(KT):
            i, w, _, token, last = next_block()
            done = pe.put(lambda e, w=w, k=k: e.matmul(bank[:, j:j + 1], w, c_act[:, k:k + 1], start=k == 0, stop=k == KT - 1),
                          token, ada["reader"], c_ready, counted=last)
        close_slab(i, done)
        if j == KT - 1:
            part = n // KT
            base = COLS["ada_b"][0] + part * KT
            ada["token"][part] = dve.put(lambda e: e.tensor_tensor(
                mod[:, part * KT:(part + 1) * KT], bank[:, 0:KT], cols[:, base:base + KT], ALU.add), done, consts_ready)
            give(bank, ada["token"][part])
        ada["n"] += 1

    for _ in range(2 * KT):
        ada_column()
    gain1_ready = dve.put(lambda e: e.scalar_tensor_tensor(gain1[:], modc(1, 0, KT), 1.0, col("norm1_g", 0, KT), ALU.add, ALU.mult),
                          ada["token"][1])
    h_ready = normed(lambda k: gain1[:, k:k + 1], lambda k: modc(0, k), [x_ready, gain1_ready], None)

    mix = ExitStack()
    gates = sb("gates", [P, 2 * KT, S], stack=mix)
    conv = sb("conv", [P, CT, S], stack=mix)
    mixed = sb("mixed", [P, CT, S], stack=mix)
    pool_w = sb("pool_w", [P, CT, P], stack=mix)
    front = ExitStack()
    p_pad = sb("p_pad", [P, CT, PAD_POOL + S], stack=front)
    a_val = sb("a_val", [P, S], stack=front)
    glu = sb("glu", [P, CT, PAD_CONV + S], stack=front)
    pooled = sb("pooled", [P, 2, PAD_POOL + S], stack=front)

    pads = pool.put(lambda e: e.memset(p_pad[:, :, 0:PAD_POOL], 0.0))
    pads = pool.put(lambda e: e.memset(glu[:, :, 0:PAD_CONV], 0.0))

    def interleave_ada():
        if ada["n"] < 44:
            ada_column()

    glu_ready = []
    a_val_reader = None
    for c in range(CT):
        bank, token = project(h_hi, h_lo, range(KT), h_ready)
        interleave_ada()
        a = act.put(lambda e, bank=bank, c=c: e.activation(a_val[:], bank[:], ACT.Identity, bias=col("b_in", CT + c)),
                    token, a_val_reader)
        give(bank, a)
        bank, token = project(h_hi, h_lo, range(KT), h_ready)
        interleave_ada()
        i, s, r = scratch()
        b = act.put(lambda e, bank=bank, s=s, c=c: e.activation(s, bank[:], ACT.Sigmoid, bias=col("b_in", 2 * CT + c)), token, r)
        give(bank, b)
        a_val_reader = dve.put(lambda e, s=s, c=c: e.tensor_tensor(glu[:, c, PAD_CONV:], a_val[:], s, ALU.mult), b, a)
        tmp_reader[i] = a_val_reader
        glu_ready.append(a_val_reader)

    conv_token = [None] * CT

    def convolve():
        for j in range(CONV_K):
            for c in range(CT):
                tap = col("dw_kernel", c * CONV_K + j)
                src = glu[:, c, j:j + S]
                if j == 0:
                    conv_token[c] = dve.put(lambda e, c=c, tap=tap, src=src: e.tensor_scalar(
                        conv[:, c, :], src, tap, col("dw_bias", c), ALU.mult, ALU.add), glu_ready[c], pads)
                else:
                    conv_token[c] = dve.put(lambda e, c=c, tap=tap, src=src: e.scalar_tensor_tensor(
                        conv[:, c, :], src, tap, conv[:, c, :], ALU.mult, ALU.add), conv_token[c])
                yield

    conv_work = convolve()
    background.append([conv_work, 4])

    p_ready = []
    for c in range(CT):
        bank, token = project(h_hi, h_lo, range(KT), h_ready)
        interleave_ada()
        a = act.put(lambda e, bank=bank, c=c: e.activation(p_pad[:, c, PAD_POOL:], bank[:], ACT.Identity, bias=col("b_in", c)), token)
        give(bank, a)
        p_ready.append(a)

    mixed_ready = []
    pool_prev = None
    for c, w in enumerate(POOL_WINDOWS):
        src, token, shift, lv = p_pad[:, c, :], [p_ready[c], pads, pool_prev], 1, 0
        lo_col = 0
        while shift < w:
            lo_col += shift
            dst = pooled[:, lv % 2, :]
            token = pool.put(lambda e, dst=dst, src=src, shift=shift, lo_col=lo_col: e.tensor_tensor(
                dst[:, lo_col:], src[:, lo_col:], src[:, lo_col - shift:PAD_POOL + S - shift], ALU.add), token)
            src, shift, lv = dst, shift * 2, lv + 1
        body = mixed[:, c, :]
        a = pool.put(lambda e, body=body, src=src, w=w: e.tensor_scalar(body, src[:, PAD_POOL:], 1.0 / w, None, ALU.mult), token)
        a = pool.put(lambda e, body=body, c=c: e.tensor_tensor(body[:, 0:PAD_POOL], body[:, 0:PAD_POOL], window_fix[:, c, :], ALU.mult),
                     a, consts_ready)
        pool_prev = pool.put(lambda e, body=body, c=c: e.tensor_tensor(body, body, p_pad[:, c, PAD_POOL:], ALU.subtract), a)
        mixed_ready.append(pool_prev)

    gate_ready = []
    for n in range(2 * KT):
        bank, token = project(h_hi, h_lo, range(KT), h_ready)
        interleave_ada()
        a = act.put(lambda e, bank=bank, n=n: e.activation(gates[:, n, :], bank[:], ACT.Sigmoid, bias=col("b_in", 3 * CT + n)), token)
        give(bank, a)
        gate_ready.append(a)
    while ada["n"] < 48:
        ada_column()
    finish(conv_work)
    h_reader = token

    pool_w_in = counter("pool_w_in")
    pool_w_ready = act.dma(pool_w[:], t["pool_w"], pool_w_in)
    front_done = [pool_prev, conv_token]
    front.close()
    b_hi = sb("b_hi", [P, KT, S], F32R, stack=mix)
    b_lo = sb("b_lo", [P, KT, S], F32R, stack=mix)
    b_ready = [None] * KT
    for c in range(CT):
        bank, reader = take()
        a = pe.put(lambda e, bank=bank, c=c: e.matmul(bank[:], pool_w[:, c, :], mixed[:, c, :], start=True, stop=True),
                   mixed_ready[c], pool_w_ready, reader)
        i, s, r = scratch()
        a = dve.put(lambda e, bank=bank, s=s, c=c: e.tensor_scalar(s, bank[:], col("pool_scale", c), None, ALU.mult), a, r)
        give(bank, a)
        b_ready[c] = tmp_reader[i] = split(s, b_hi[:, c, :], b_lo[:, c, :], a, front_done)

    bank, token = feature_sum([conv[:, c, :] for c in range(CT)], conv_token, square=False)
    for c in range(CT):
        a = dve.put(lambda e, bank=bank, c=c: e.scalar_tensor_tensor(conv[:, c, :], bank[:], -1.0 / CW, conv[:, c, :], ALU.mult, ALU.add), token)
    give(bank, a)
    bank, token = feature_sum([conv[:, c, :] for c in range(CT)], a)
    r = inverse_root(bank, token, CW)
    for c in range(CT):
        a = dve.put(lambda e, c=c: e.scalar_tensor_tensor(conv[:, c, :], conv[:, c, :], col("conv_ln_g", c), rstd[:], ALU.mult, ALU.mult), r)
        rstd_reader[0] = a
        i, s, rd = scratch()
        b = act.put(lambda e, c=c, s=s: e.activation(s, conv[:, c, :], ACT.Silu, bias=col("conv_ln_b", c)), a, rd)
        b_ready[CT + c] = tmp_reader[i] = split(s, b_hi[:, CT + c, :], b_lo[:, CT + c, :], b, front_done)

    merged_ready = []
    for n in range(KT):
        bank_p, token_p = project(b_hi, b_lo, range(CT), b_ready[:CT])
        bank_c, token_c = project(b_hi, b_lo, range(CT, KT), b_ready[CT:])
        i, s, r = scratch()
        a = dve.put(lambda e, s=s, n=n, bank=bank_p: e.tensor_tensor(s, bank[:], gates[:, n, :], ALU.mult), token_p, r, gate_ready[n])
        give(bank_p, a)
        i2, s2, r2 = scratch()
        b = dve.put(lambda e, s2=s2, n=n, bank=bank_c: e.tensor_tensor(s2, bank[:], gates[:, KT + n, :], ALU.mult), token_c, r2, gate_ready[KT + n])
        give(bank_c, b)
        c_ = pool.put(lambda e, s=s, s2=s2: e.tensor_tensor(s, s, s2, ALU.add), a, b)
        tmp_reader[i2] = c_
        done = split(s, h_hi[:, n, :], h_lo[:, n, :], c_, h_reader)
        tmp_reader[i] = done
        merged_ready.append(done)

    x_tokens = []
    for n in range(KT):
        bank, token = project(h_hi, h_lo, range(KT), merged_ready)
        a = dve.put(lambda e, bank=bank, n=n: e.scalar_tensor_tensor(x[:, n, :], bank[:], modc(2, n), x[:, n, :], ALU.mult, ALU.add), token)
        give(bank, a)
        x_tokens.append(a)
    mix_done = [token, a, pool_prev, act.put(lambda e: e.copy(gain2[:], gain1[:]))]
    mix.close()

    gain2_ready = dve.put(lambda e: e.scalar_tensor_tensor(gain2[:], modc(4, 0, KT), 1.0, col("norm2_g", 0, KT), ALU.add, ALU.mult),
                          mix_done)
    h_ready = normed(lambda k: gain2[:, k:k + 1], lambda k: modc(3, k), [x_tokens[-1], gain2_ready], token)

    peer = ExitStack()
    keys = sb("keys", [P, 2, P], stack=peer)
    q_t = sb("q_t", [P, 2, S], stack=peer)
    top = sb("top", [P, TT, 2, TOPK], stack=peer)
    top_u = sb("top_u", [P, TT, 2, TOPK], U32, stack=peer)
    top_f = sb("top_f", [P, TT, 2, TOPK], stack=peer)
    rest = sb("rest", [P, 2 * P], stack=peer)
    cand = sb("cand", [P, TT, TOPK, TOPK], stack=peer)
    pos = sb("pos", [P, TT, TOPK], U32, stack=peer)
    pos_u = sb("pos_u", [P, 2, TT, TOPK], U32, stack=peer)
    pos_f = sb("pos_f", [P, 2, TT, TOPK], stack=peer)
    sel_s = sb("sel_s", [P, TT, HEADS, TOPK], stack=peer)
    sel_i = sb("sel_i", [P, 2, TT, HEADS, TOPK], stack=peer)
    soft = sb("soft", [P, TT * HEADS], stack=peer)
    sel_t = sb("sel_t", [P, 3, S], stack=peer)
    hot2 = sb("hot2", [P, 2, TOK4, P], stack=peer)
    hot1 = sb("hot1", [P, 2, TOK4, P], stack=peer)
    gelu = sb("gelu", [P, GELU_SLOTS, S], stack=peer)
    g_tile = sb("g_tile", [P, G_SLOTS, S], stack=peer)
    staging = ExitStack()
    stage_all = sb("stage", [P, P, CHUNK], stack=staging)
    keys_in = counter("keys_in")
    keys_ready = act.dma(keys[:], t["keys"], keys_in, *mix_done)

    routed = []

    q_reader = [None]

    def route(h):
        bank_of = []
        for half in range(2):
            bank, reader = take()
            for tt in range(TT):
                a = pe.put(lambda e, bank=bank, half=half, tt=tt: e.matmul(
                    bank[:, tt * P:(tt + 1) * P], q_t[:, half, tt * P:(tt + 1) * P], keys[:, half, :], start=True, stop=True),
                    q_ready[half], reader, keys_ready, mix_done)
            bank_of.append((bank, a))
        q_reader[0] = a
        last = None
        for half in range(2):
            bank, token = bank_of[half]
            for tt in range(TT):
                s = bank[:, tt * P:(tt + 1) * P]
                v, u = top[:, tt, half, :], top_u[:, tt, half, :]
                a = dve.put(lambda e, s=s, v=v: e.max(v[:, 0:8], s), token, routed[-1:] or mix_done)
                b = dve.put(lambda e, s=s, v=v: e.match_replace(rest[:, 0:P], v[:, 0:8], s, NEG), a)
                c = dve.put(lambda e, s=s, v=v, u=u: e.max_index(u[:, 0:8], v[:, 0:8], s), a)
                a = dve.put(lambda e, v=v: e.max(v[:, 8:16], rest[:, 0:P]), b)
                last = dve.put(lambda e, v=v, u=u: e.max_index(u[:, 8:16], v[:, 8:16], rest[:, 0:P]), a)
                yield
            give(bank, last)
        top_ready = dve.put(lambda e: e.tensor_copy(top_f[:], top_u[:]), last)
        one = top[:, :, 0, :].unsqueeze(3).to_broadcast([P, TT, TOPK, TOPK])
        two = top[:, :, 1, :].unsqueeze(2).to_broadcast([P, TT, TOPK, TOPK])
        cand_ready = dve.put(lambda e: e.tensor_tensor(cand[:], one, two, ALU.add), last)
        yield
        for tt in range(TT):
            s = cand[:, tt, :, :].rearrange("p a b -> p (a b)")
            v, u = sel_s[:, tt, h, :], pos[:, tt, :]
            a = dve.put(lambda e, s=s, v=v: e.max(v[:, 0:8], s), cand_ready)
            b = dve.put(lambda e, s=s, v=v: e.match_replace(rest[:], v[:, 0:8], s, NEG), a)
            c = dve.put(lambda e, s=s, v=v, u=u: e.max_index(u[:, 0:8], v[:, 0:8], s), a)
            a = dve.put(lambda e, v=v: e.max(v[:, 8:16], rest[:]), b)
            last = dve.put(lambda e, v=v, u=u: e.max_index(u[:, 8:16], v[:, 8:16], rest[:]), a)
            yield
        a = dve.put(lambda e: e.tensor_single_scalar(pos_u[:, 0], pos[:], 4, ALU.logical_shift_right), last)
        b = dve.put(lambda e: e.tensor_single_scalar(pos_u[:, 1], pos[:], TOPK - 1, ALU.bitwise_and), last)
        pos_ready = dve.put(lambda e: e.tensor_copy(pos_f[:], pos_u[:]), b)
        yield
        iota_b = iota16[:].unsqueeze(1).unsqueeze(1).to_broadcast([P, TT, TOPK, TOPK])
        for half in range(2):
            pf = pos_f[:, half].unsqueeze(3).to_broadcast([P, TT, TOPK, TOPK])
            tf = top_f[:, :, half, :].unsqueeze(2).to_broadcast([P, TT, TOPK, TOPK])
            a = dve.put(lambda e, pf=pf: e.tensor_tensor(cand[:], pf, iota_b, ALU.is_equal), pos_ready, consts_ready, top_ready, last)
            a = dve.put(lambda e, tf=tf: e.tensor_tensor(cand[:], cand[:], tf, ALU.mult), a)
            last = dve.put(lambda e, half=half: e.tensor_reduce(sel_i[:, half, :, h, :], cand[:], AX_X, ALU.add), a)
            yield
        routed.append(last)

    route_work = []
    for h in range(HEADS):
        q_ready = []
        for half in range(2):
            bank, token = project(h_hi, h_lo, range(KT), h_ready)
            a = act.put(lambda e, bank=bank, half=half: e.copy(q_t[:, half, :], bank[:]), token, q_reader[0], mix_done)
            give(bank, a)
            q_ready.append(a)
        if route_work:
            finish(route_work[-1])
        work = route(h)
        route_work.append(work)
        next(work)
        background.append([work, 7])

    gelu_reader = [mix_done] * GELU_SLOTS
    gelu_ready = {}

    def expert_up(b):
        bank, token = project(h_hi, h_lo, range(KT), h_ready)
        s = b % GELU_SLOTS
        gelu_ready[b] = act.put(lambda e, bank=bank, s=s: e.activation(gelu[:, s, :], bank[:], ACT.Gelu_apprx_tanh), token, gelu_reader[s])
        give(bank, gelu_ready[b])

    g_dram = t["g_scratch"]
    chunk_out = counter("chunk_out")

    def routing_matrix():
        v = sel_s[:].rearrange("p t h k -> p (t h) k")
        best = sel_s[:, :, :, 0:1].rearrange("p t h k -> p (t h) k").to_broadcast([P, TT * HEADS, TOPK])
        e_ = cand[:].rearrange("p t a b -> p (t a b)")[:, 0:TT * HEADS * TOPK].rearrange("p (g k) -> p g k", k=TOPK)
        a = dve.put(lambda e: e.tensor_tensor(e_, v, best, ALU.subtract), routed[-1])
        a = act.put(lambda e: e.activation(e_, e_, ACT.Exp), a)
        b = dve.put(lambda e: e.tensor_reduce(soft[:], e_, AX_X, ALU.add), a)
        b = dve.put(lambda e: e.reciprocal(soft[:], soft[:]), b)
        gate = dve.put(lambda e: e.tensor_tensor(v, e_, soft[:].unsqueeze(2).to_broadcast([P, TT * HEADS, TOPK]), ALU.mult), b)
        yield
        sel_ready = []
        for n, src in enumerate((sel_s[:], sel_i[:, 0], sel_i[:, 1])):
            bank, reader = take()
            for tt in range(TT):
                a = pe.put(lambda e, bank=bank, tt=tt, src=src: e.transpose(
                    bank[:, tt * P:(tt + 1) * P], src[:, tt].rearrange("p h k -> p (h k)"), ident[:]), gate, reader, consts_ready)
            a = act.put(lambda e, bank=bank, n=n: e.copy(sel_t[:, n, :], bank[:]), a)
            give(bank, a)
            sel_ready.append(a)
        yield
        hot_reader = [None, None]
        chunk_token = None
        chunk_done = None
        for g in range(S // TOK4):
            r, t0 = g % 2, g * TOK4
            for j in range(TOK4):
                a = pool.put(lambda e, r=r, j=j, t0=t0: e.tensor_scalar(
                    hot2[:, r, j, :], iota128[:], sel_t[:, 2, t0 + j:t0 + j + 1], None, ALU.is_equal), sel_ready, hot_reader[r])
                b = dve.put(lambda e, r=r, j=j, t0=t0: e.tensor_scalar(
                    hot1[:, r, j, :], iota128[:], sel_t[:, 1, t0 + j:t0 + j + 1], sel_t[:, 0, t0 + j:t0 + j + 1],
                    ALU.is_equal, ALU.mult), sel_ready, hot_reader[r])
            bank, reader = take()
            for j in range(TOK4):
                c = pe.put(lambda e, bank=bank, r=r, j=j: e.matmul(
                    bank[:, j * P:(j + 1) * P], hot2[:, r, j, :], hot1[:, r, j, :], start=True, stop=True), a, b, reader)
            hot_reader[r] = c
            o = t0 % CHUNK
            chunk_token = act.put(lambda e, bank=bank, o=o: e.copy(
                stage_all[:, :, o:o + TOK4].rearrange("p b t -> p t b"), bank[:].rearrange("p (t b) -> p t b", t=TOK4)), c, chunk_done)
            give(bank, chunk_token)
            if o + TOK4 == CHUNK:
                c0 = t0 + TOK4 - CHUNK
                chunk_done = act.dma(g_dram[:, :, c0:c0 + CHUNK].rearrange("b p t -> p b t"), stage_all[:], chunk_out, chunk_token)
            yield
        g_written.append(chunk_done)

    g_written = []
    matrix_work = routing_matrix()
    for b in range(GELU_SLOTS):
        expert_up(b)
        if b == 5:
            finish(route_work[-1])
            background.append([matrix_work, 18])
    finish(route_work[-1])
    finish(matrix_work)

    staging.close()
    act_hi = sb("act_hi", [P, GROUP, S], F32R, stack=peer)
    act_lo = sb("act_lo", [P, GROUP, S], F32R, stack=peer)
    g_in = [counter(f"g_in{i}") for i in range(G_SLOTS)]
    g_reader = [g_written[-1]] * G_SLOTS
    g_landed = {}
    w_ready = {}
    v_last = [None]

    def load_g(b):
        if b < EXPERT_TILES:
            s = b % G_SLOTS
            g_landed[b] = sp.dma(g_tile[:, s, :], g_dram[b], g_in[s], g_written[-1], g_reader[s])

    def weigh(b):
        s, gs = b % GELU_SLOTS, b % G_SLOTS
        src = gelu[:, s, :]
        a = dve.put(lambda e, src=src, gs=gs: e.tensor_tensor(src, src, g_tile[:, gs, :], ALU.mult), gelu_ready[b], g_landed[b])
        g_reader[gs] = a
        load_g(b + G_SLOTS)
        k = b % GROUP
        w_ready[b] = gelu_reader[s] = split(src, act_hi[:, k, :], act_lo[:, k, :], a, v_last[0], g_written[-1])

    for b in range(G_SLOTS):
        load_g(b)
    for b in range(GROUP):
        weigh(b)
    u_next = GELU_SLOTS
    for g in range(N_GROUPS):
        ready_w = [w_ready[g * GROUP + j] for j in range(GROUP)]
        for dt in range(KT):
            bank, token = project(act_hi, act_lo, range(GROUP), ready_w)
            x_tokens[dt] = dve.put(lambda e, bank=bank, dt=dt: e.scalar_tensor_tensor(
                x[:, dt, :], bank[:], modc(5, dt), x[:, dt, :], ALU.mult, ALU.add), token, x_tokens[dt])
            give(bank, x_tokens[dt])
        v_last[0] = token
        for j in range(GROUP):
            if u_next < EXPERT_TILES:
                expert_up(u_next)
                u_next += 1
            if g + 1 < N_GROUPS:
                weigh((g + 1) * GROUP + j)
    peer_done = [token, x_tokens[-1], (act, act.count), (pool, pool.count)]
    peer.close()

    def norm_in_place(name, token):
        bank, token2 = feature_sum([x[:, k, :] for k in range(KT)], token)
        r = inverse_root(bank, token2, D)
        for k in range(KT):
            a = dve.put(lambda e, k=k: e.scalar_tensor_tensor(x[:, k, :], x[:, k, :], col(name, k), rstd[:], ALU.mult, ALU.mult), r, token)
        rstd_reader[0] = a
        return a

    x_done = norm_in_place("final_g", peer_done)

    def swiglu(norm_name, x_token, h_reader):
        hr = normed(lambda k: col(norm_name, k), None, x_token, h_reader)
        with ExitStack() as ffn:
            f_hi = sb(norm_name + "_f_hi", [P, FT, S], F32R, stack=ffn)
            f_lo = sb(norm_name + "_f_lo", [P, FT, S], F32R, stack=ffn)
            f_ready = None
            for n in range(FT):
                bank_g, token_g = project(h_hi, h_lo, range(KT), hr)
                bank_u, token_u = project(h_hi, h_lo, range(KT), hr)
                i, s, r = scratch()
                a = act.put(lambda e, s=s, bank=bank_g: e.activation(s, bank[:], ACT.Silu), token_g, r)
                give(bank_g, a)
                b = dve.put(lambda e, s=s, bank=bank_u: e.tensor_tensor(s, s, bank[:], ALU.mult), token_u, a)
                give(bank_u, b)
                f_ready = tmp_reader[i] = split(s, f_hi[:, n, :], f_lo[:, n, :], b, x_token)
            for n in range(KT):
                bank, token = project(f_hi, f_lo, range(FT), f_ready)
                a = dve.put(lambda e, bank=bank, n=n: e.scalar_tensor_tensor(x[:, n, :], bank[:], 0.5, x[:, n, :], ALU.mult, ALU.add), token)
                give(bank, a)
        return a, token_u, token

    x_done, h_reader, f_reader = swiglu("ffn1_norm_2", x_done, peer_done[0])

    att = ExitStack()
    qk_t = sb("qk_t", [P, 16, S], stack=att)
    v_nat = sb("v_nat", [P, TT, D], stack=att)
    bias = sb("bias", [P, 4, S], stack=att)
    mult = sb("mult", [P, S], stack=att)
    lam_in = sb("lam_in", [P, 4, DH], stack=att)
    lam = sb("lam", [P, 8], stack=att)
    stat = sb("stat", [P, 8 * N_MAPS], stack=att)
    tables = ExitStack()
    table = sb("table", [DH, N_MAPS], stack=tables)
    buckets = sb("buckets", [DH, 2, BIAS_L], stack=tables)
    by_dist = sb("by_dist", [DIL_HEADS, 2, BIAS_L], stack=tables)
    att_in = counter("att_in")
    bias_out = counter("bias_out")
    bias_in = [counter(f"bias_in{i}") for i in range(4)]

    old = [x_done, f_reader, (act, act.count)]
    for dst, name in ((table, "rel_bias"), (buckets, "buckets"), (mult, "mult"), (lam_in, "lam_in")):
        att_ready = sp.dma(dst[:], t[name], att_in, *old)
    bank_pair = [take(), take()]
    for m, (width, off) in enumerate(((S, 0), (BIAS_L - S, S))):
        for kind in range(2):
            bank, reader = (take() if (m, kind) != (0, 0) else bank_pair[0])
            a = pe.put(lambda e, bank=bank, kind=kind, off=off, width=width: e.matmul(
                bank[0:DIL_HEADS, 0:width], table[:, kind * 8:kind * 8 + 8], buckets[:, kind, off:off + width],
                start=True, stop=True), att_ready, reader)
            a = act.put(lambda e, bank=bank, kind=kind, off=off, width=width: e.copy(
                by_dist[:, kind, off:off + width], bank[0:DIL_HEADS, 0:width]), a)
            give(bank, a)
    free_banks.append(bank_pair[1])
    b_dram = t["bias_scratch"]
    for kind in range(2):
        b_out = act.dma(b_dram[:, kind * 8:kind * 8 + 8, :].rearrange("q m x -> m q x"),
                        by_dist[:, kind, :].unsqueeze(1).to_broadcast([DIL_HEADS, P, BIAS_L]), bias_out, a)
    bias_reader = [old] * 4
    bias_ready = {}

    def load_bias(m):
        if m < N_MAPS:
            skew = bass.AP(b_dram.tensor, m * BIAS_L + P - 1, [[N_MAPS * BIAS_L - 1, P], [1, S]])
            bias_ready[m] = pool.dma(bias[:, m % 4, :], skew, bias_in[m % 4], b_out, bias_reader[m % 4])

    for m in range(4):
        load_bias(m)
    tables.close()

    a = dve.put(lambda e: e.tensor_tensor(lam_in[:, 0:2, :], lam_in[:, 0:2, :], lam_in[:, 2:4, :], ALU.mult), att_ready)
    a = dve.put(lambda e: e.tensor_reduce(lam[:, 0:2], lam_in[:, 0:2, :], AX_X, ALU.add), a)
    a = act.put(lambda e: e.activation(lam[:, 2:4], lam[:, 0:2], ACT.Exp), a)
    a = dve.put(lambda e: e.tensor_tensor(lam[:, 4:5], lam[:, 2:3], lam[:, 3:4], ALU.subtract), a)
    a = dve.put(lambda e: e.tensor_scalar(lam[:, 5:6], lam[:, 4:5], LAM0, None, ALU.add), a)
    lam_ready = dve.put(lambda e: e.tensor_scalar(subln[:], col("subln_gain_2", 0), 1.0 - LAM0, None, ALU.mult), a)

    h_ready = normed(lambda k: col("mix_norm_2", k), None, x_done, h_reader)
    qk_ready = [None] * 16
    for n in range(16):
        bank, token = project(h_hi, h_lo, range(KT), h_ready)
        qk_ready[n] = act.put(lambda e, bank=bank, n=n: e.copy(qk_t[:, n, :], bank[:]), token, old)
        give(bank, qk_ready[n])
    v_ready = None
    for half in range(2):
        four = [take() for _ in range(TT)]
        for k in range(KT):
            i, w_h, w_l, token, last = next_block(4)
            for tt in range(TT):
                cut = slice(tt * P, (tt + 1) * P)
                done = three(four[tt][0][:], h_hi[:, k, cut], h_lo[:, k, cut], w_h, w_l, k == 0, k == KT - 1,
                             token, four[tt][1] if k == 0 else None)
            if last:
                close_slab(i, done)
        for tt in range(TT):
            v_ready = act.put(lambda e, bank=four[tt][0], tt=tt, half=half: e.copy(v_nat[:, tt, half * S:(half + 1) * S], bank[:]), done, old)
            give(four[tt][0], v_ready)
    h_reader = done

    maps = [(c, 4 + c, DH * m, 2 * c + m) for c in range(DIFF_HEADS) for m in range(2)]
    maps += [(8 + h // 2, 12 + h // 2, DH * (h % 2), 8 + h) for h in range(DIL_HEADS)]
    probs_turn = [0]
    probs_reader = [None, None]
    prob_t_reader = [None]
    stat_n = [0]

    probs = sb("probs", [P, 2, 2, S], stack=att)
    prob_t = sb("prob_t", [P, TT, S], stack=att)
    place_free = [b_out]

    def attend(map_ids, qt, slot_reader, slot):
        width = (qt + 1) * P
        ready = []
        for m, mid in enumerate(map_ids):
            qi, ki, off, bc = maps[mid]
            rows = slice(off, off + DH)
            bank, reader = take()
            a = pe.put(lambda e: e.matmul(bank[:, 0:width], qk_t[rows, qi, qt * P:(qt + 1) * P], qk_t[rows, ki, 0:width],
                                          start=True, stop=True), qk_ready[qi], qk_ready[ki], reader)
            w = probs[:, slot, m, 0:width]
            k = 2 * stat_n[0]
            stat_n[0] = (stat_n[0] + 1) % (4 * N_MAPS)
            top_c, sum_c = stat[:, k:k + 1], stat[:, k + 1:k + 2]
            a = dve.put(lambda e: e.scalar_tensor_tensor(w, bank[:, 0:width], DH ** -0.5, bias[:, bc % 4, S - width:S], ALU.mult, ALU.add),
                        a, bias_ready[bc], slot_reader, old, place_free)
            bias_reader[bc % 4] = a
            if qt == TT - 1:
                load_bias(bc + 4)
            give(bank, a)
            b = dve.put(lambda e: e.tensor_reduce(top_c, w, AX_X, ALU.max), a)
            b = dve.put(lambda e: e.tensor_scalar(top_c, top_c, -1.0, None, ALU.mult), b)
            if len(map_ids) == 2:
                b = act.put(lambda e: e.activation(w, w, ACT.Exp, bias=top_c, accum_out=sum_c), b)
            else:
                b = act.put(lambda e: e.activation(w, w, ACT.Exp, bias=top_c), b)
                b = dve.put(lambda e: e.tensor_tensor(w, w, mult[:, S - width:S], ALU.mult), b)
                b = dve.put(lambda e: e.tensor_reduce(sum_c, w, AX_X, ALU.add), b)
            b = dve.put(lambda e: e.reciprocal(sum_c, sum_c), b)
            ready.append((w, sum_c, b))
        w0, s0, b0 = ready[0]
        if len(map_ids) == 1:
            return dve.put(lambda e: e.tensor_scalar(w0, w0, s0, None, ALU.mult), b0)
        w1, s1, b1 = ready[1]
        c = dve.put(lambda e: e.tensor_tensor(s1, s1, lam[:, 5:6], ALU.mult), b1, lam_ready)
        d = dve.put(lambda e: e.tensor_scalar(w0, w0, s0, None, ALU.mult), b0)
        c = dve.put(lambda e: e.tensor_scalar(w1, w1, s1, None, ALU.mult), c)
        return dve.put(lambda e: e.tensor_tensor(w0, w0, w1, ALU.subtract), c, d)

    def transposed(map_ids):
        four = [take() for _ in range(TT)]
        done = [None] * TT
        for qt in range(TT):
            slot = probs_turn[0] % 2
            probs_turn[0] += 1
            a = attend(map_ids, qt, probs_reader[slot], slot)
            for kt in range(qt + 1):
                done[kt] = pe.put(lambda e, kt=kt, qt=qt, slot=slot: e.transpose(
                    four[kt][0][:, qt * P:(qt + 1) * P], probs[:, slot, 0, kt * P:(kt + 1) * P], ident[:]), a, four[kt][1])
            probs_reader[slot] = done[qt]
        out = []
        for kt in range(TT):
            a = act.put(lambda e, kt=kt: e.copy(prob_t[:, kt, kt * P:], four[kt][0][:, kt * P:]), done[kt], prob_t_reader[0], place_free)
            give(four[kt][0], a)
            out.append(a)
        return out

    b_ready = [None] * KT
    for c in range(DIFF_HEADS):
        ready_t = transposed([2 * c, 2 * c + 1])
        bank, reader = take()
        for kt in range(TT):
            a = pe.put(lambda e, kt=kt, bank=bank, c=c: e.matmul(bank[:, kt * P:], v_nat[:, kt, c * P:(c + 1) * P], prob_t[:, kt, kt * P:],
                                                                 start=kt == 0, stop=kt == TT - 1), ready_t[kt], v_ready, reader)
        prob_t_reader[0] = a
        i, s, r = scratch()
        a = act.put(lambda e, s=s, bank=bank: e.copy(s, bank[:]), a, r)
        give(bank, a)
        bank, token = feature_sum([s], a)
        r = inverse_root(bank, token, P)
        a = dve.put(lambda e, s=s: e.scalar_tensor_tensor(s, s, subln[:, 0:1], rstd[:], ALU.mult, ALU.mult), r, lam_ready)
        rstd_reader[0] = a
        b_ready[c] = tmp_reader[i] = split(s, h_hi[:, c, :], h_lo[:, c, :], a, h_reader)
    for pair in range(DIL_HEADS // 2):
        bank, reader = take()
        for m in range(2):
            h = 2 * pair + m
            ready_t = transposed([8 + h])
            out_rows = slice(DH * m, DH * (m + 1))
            for kt in range(TT):
                a = pe.put(lambda e, kt=kt, bank=bank, h=h, out_rows=out_rows: e.matmul(
                    bank[out_rows, kt * P:], v_nat[:, kt, S + h * DH:S + (h + 1) * DH], prob_t[:, kt, kt * P:],
                    start=kt == 0, stop=kt == TT - 1), ready_t[kt], v_ready, reader)
            prob_t_reader[0] = a
        i, s, r = scratch()
        a = act.put(lambda e, s=s, bank=bank: e.copy(s, bank[:]), a, r)
        give(bank, a)
        b_ready[DIFF_HEADS + pair] = tmp_reader[i] = split(s, h_hi[:, DIFF_HEADS + pair, :], h_lo[:, DIFF_HEADS + pair, :], a, h_reader)

    for n in range(KT):
        bank, token = project(h_hi, h_lo, range(KT), b_ready)
        a = dve.put(lambda e, bank=bank, n=n: e.tensor_tensor(x[:, n, :], bank[:], x[:, n, :], ALU.add), token)
        give(bank, a)
    x_done = [a, token, (act, act.count), (dve, dve.count)]
    att.close()

    x_done, h_reader, f_reader = swiglu("ffn2_norm_2", x_done, token)
    x_done = norm_in_place("final_norm_2", x_done)
    out_done = counter("out_done")
    stored = sp.dma(t["out"], x[:], out_done, x_done)
    sp.wait(stored)
    sp.wait((chunk_out, chunk_out.count))
    sp.wait((bias_out, bias_out.count))
    assert used[0] == len(order), (used[0], len(order))
    nc.all_engine_barrier()


def slabs(w):
    k, n = w.shape
    b = w.reshape(k // P, P, n // P, P).transpose(2, 0, 1, 3).reshape(-1, SLAB, P, P)
    return np.ascontiguousarray(b.transpose(0, 2, 1, 3).reshape(-1, P, SLAB * P))


def wide_slabs(w):
    b = w.reshape(w.shape[0] // (2 * P), 2, P, w.shape[1])
    return np.ascontiguousarray(b.transpose(0, 2, 1, 3).reshape(-1, P, SLAB * P))


def columns(v):
    return v.reshape(-1, P).T


def bucket_of(dist):
    n = np.maximum(dist, 0)
    nf = np.maximum(n, 1).astype(np.float32)
    large = 16 + (np.log(nf / 16) / math.log(2048 / 16) * 16).astype(np.int32)
    return np.where(n < 16, n, np.minimum(large, 31))


def windows_of(dist):
    n = sum(((dist >= 0) & (dist % r == 0) & (dist <= w)).astype(np.int32) for w, r in ((128, 1), (512, 4), (2048, 16)))
    return n


def constants():
    i = np.arange(P, dtype=np.float32)
    fix = np.ones((P, CT, PAD_POOL), np.float32)
    for c, w in enumerate(POOL_WINDOWS):
        fix[:, c, :] = w / np.minimum(np.arange(1, PAD_POOL + 1), w)
    dist = S - 1 - np.arange(BIAS_L)
    buckets = np.zeros((DH, 2, BIAS_L), np.float32)
    for kind in range(2):
        buckets[bucket_of(dist), kind, np.arange(BIAS_L)] = 1.0
        buckets[32, kind, :] = (dist < 0) if kind == 0 else (windows_of(dist) == 0)
    z = np.arange(P)[:, None] + (S - P) - np.arange(S)[None, :]
    return {
        "ident": np.eye(P, dtype=np.float32),
        "ones": np.ones((P, P), np.float32),
        "iota128": np.ascontiguousarray(np.broadcast_to(i, (P, P))),
        "iota16": np.ascontiguousarray(np.broadcast_to(i[:TOPK], (P, TOPK))),
        "window_fix": fix,
        "buckets": buckets,
        "mult": windows_of(z).astype(np.float32),
    }


def laid_out(a):
    o = dict(constants())
    o["x"] = np.ascontiguousarray(a["x"][0].T.reshape(KT, P, S).transpose(1, 0, 2))
    vectors = {n: columns(a[n].reshape(-1)) for n in COLS if n != "dw_kernel"}
    vectors["dw_kernel"] = a["dw_kernel"][0].T.reshape(CT, P, CONV_K).transpose(1, 0, 2).reshape(P, -1)
    o["cols"] = np.ascontiguousarray(np.concatenate([vectors[n] for n in COLS], axis=1))
    o["ada_w"] = slabs(a["ada_w"][0])
    w = a["w_in"][0]
    value_gate = [w[:, CW + half * CW + c * P:CW + half * CW + (c + 1) * P] for c in range(CT) for half in range(2)]
    o["w_in"] = slabs(np.concatenate(value_gate + [w[:, :CW], w[:, 3 * CW:]], axis=1))
    o["pool_w"] = np.ascontiguousarray(a["pool_w"][0].transpose(1, 0, 2))
    o["w_merge"] = slabs(np.concatenate([a["pool_up"][0], a["conv_out"][0]], axis=0))
    o["w_out"] = slabs(a["w_out"][0])
    o["w_query"] = slabs(a["w_query"][0])
    o["keys"] = np.ascontiguousarray(np.stack([a["sub_keys_1"][0].T, a["sub_keys_2"][0].T], axis=1))
    u = a["expert_u"][0].reshape(EXPERT_TILES, P, KT, P)
    o["expert_u"] = np.ascontiguousarray(u.transpose(0, 3, 2, 1).reshape(EXPERT_TILES, P, KT * P))
    v = a["expert_v"][0].reshape(N_GROUPS, GROUP, P, KT, P)
    o["expert_v"] = np.ascontiguousarray(v.transpose(0, 3, 2, 1, 4).reshape(N_GROUPS * KT, P, GROUP * P))
    for n in ("ffn1", "ffn2"):
        g = a[f"{n}_w_gate_2"][0].reshape(D, FT, P)
        up = a[f"{n}_w_up_2"][0].reshape(D, FT, P)
        o[f"{n}_gate_up"] = slabs(np.stack([g, up], axis=2).reshape(D, 2 * D_FF))
        o[f"{n}_down"] = slabs(a[f"{n}_w_down_2"][0])
    w = a["w_in_2"][0]
    qa, ka, va, qb, kb, vb = (w[:, i * CW:(i + 1) * CW] for i in range(6))
    o["w_in_2"] = np.concatenate([slabs(np.concatenate([qa, ka, qb, kb], axis=1)), wide_slabs(va), wide_slabs(vb)])
    o["w_out_2"] = slabs(a["w_out_2"][0])
    lam = np.stack([a["lambda_q1_2"][0], a["lambda_q2_2"][0], a["lambda_k1_2"][0], a["lambda_k2_2"][0]])
    o["lam_in"] = np.ascontiguousarray(np.broadcast_to(lam, (P, 4, DH)))
    table = np.zeros((DH, N_MAPS), np.float32)
    table[:32] = a["rel_bias_2"]
    table[32] = NEG
    o["rel_bias"] = table
    return o


def kernel(**inputs):
    import concourse.bacc as bacc
    from concourse.bass_utils import run_bass_kernel_spmd

    arrays = laid_out({n: np.asarray(v) for n, v in inputs.items()})
    nc = bacc.Bacc("TRN2", target_bir_lowering=False, num_devices=1)
    t = {n: nc.dram_tensor(n + "_dram", v.shape, F32, kind="ExternalInput").ap() for n, v in arrays.items()}
    t["out"] = nc.dram_tensor("out_dram", (P, KT, S), F32, kind="ExternalOutput").ap()
    t["g_scratch"] = nc.dram_tensor("g_scratch", (EXPERT_TILES, P, S), F32, kind="Internal").ap()
    t["bias_scratch"] = nc.dram_tensor("bias_scratch", (P, N_MAPS, BIAS_L), F32, kind="Internal").ap()
    build(nc, t)
    r = run_bass_kernel_spmd(nc, [{n + "_dram": v for n, v in arrays.items()}], core_ids=[0])
    out = r.results[0]["out_dram"]
    return np.ascontiguousarray(out.transpose(2, 1, 0).reshape(1, S, D))
```

```python
import math
from collections import deque
from contextlib import ExitStack

import numpy as np

import concourse.bass as bass
from concourse import mybir

F32 = mybir.dt.float32
F32R = mybir.dt.float32r
U32 = mybir.dt.uint32
ALU = mybir.AluOpType
ACT = mybir.ActivationFunctionType
AX_X = mybir.AxisListType.X

P = 128
S = 512
D = 1024
KT = D // P
TT = S // P
POOL_WINDOWS = (2, 4, 8, 16)
PAD_POOL = 16
CONV_K = 31
PAD_CONV = CONV_K - 1
CW = 512
CT = CW // P
HEADS = 8
TOPK = 16
N_KEYS = 128
EXPERT_TILES = N_KEYS
GROUP = 8
N_GROUPS = EXPERT_TILES // GROUP
D_FF = 256 * ((8 * D // 3 + 255) // 256)
FT = D_FF // P
DH = 64
DIFF_HEADS = 4
DIL_HEADS = 8
N_MAPS = 2 * DIFF_HEADS + DIL_HEADS
LAM0 = 0.8 - 0.6 * math.exp(-0.3 * 0)
EPS = 1e-6
NEG = -1.0e30
BIAS_L = 640
SLAB = 8
RAW_SLOTS = 6
SPLIT_SLOTS = 4
SPLIT_AHEAD = 2
GELU_SLOTS = 15
UP_PER_HEAD = (1, 1, 1, 1, 1, 1, 1, 2)
UP_EVERY = 2
HOT_SLOTS = 3
G_TILES = 4
G_SLOTS = 2
CHUNK = 32
TOK4 = 4

COLS = {}
_n = 0
for _name, _w in (("c", 8), ("ada_b", 48), ("norm1_g", 8), ("b_in", 28), ("pool_scale", 4), ("dw_bias", 4),
                  ("conv_ln_g", 4), ("conv_ln_b", 4), ("norm2_g", 8), ("final_g", 8), ("ffn1_norm_2", 8),
                  ("mix_norm_2", 8), ("ffn2_norm_2", 8), ("final_norm_2", 8), ("subln_gain_2", 1),
                  ("dw_kernel", CT * CONV_K)):
    COLS[_name] = (_n, _w)
    _n += _w
N_COLS = _n


class Queue:

    def __init__(self, engine, sem):
        self.engine, self.sem, self.count, self.waited = engine, sem, 0, {}

    def put(self, make, *after, counted=True):
        self.wait(*after)
        instruction = make(self.engine)
        if counted:
            self.count += 1
            instruction.then_inc(self.sem, 1)
        return (self, self.count)

    def wait(self, *after):
        for token in after:
            if token is None:
                continue
            if isinstance(token, list):
                self.wait(*token)
                continue
            source, value = token
            if value > self.waited.get(source, 0):
                self.waited[source] = value
                self.engine.wait_ge(source.sem, value)

    def dma(self, dst, src, counter, *after):
        self.wait(*after)
        counter.count += 16
        self.engine.dma_start(dst, src).then_inc(counter.sem, 16)
        return (counter, counter.count)


class Counter:

    def __init__(self, sem):
        self.sem, self.count = sem, 0


def build(nc, t):
    ctx = ExitStack()
    with ctx:
        program(nc, t, ctx)


def program(nc, t, ctx):
    def sb(name, shape, dt=F32, stack=ctx):
        return stack.enter_context(nc.sbuf_tensor(name, shape, dt))

    def sem(name):
        return ctx.enter_context(nc.semaphore(name))

    def counter(name):
        return Counter(sem(name))

    pe = Queue(nc.tensor, sem("pe_done"))
    act = Queue(nc.scalar, sem("act_done"))
    dve = Queue(nc.vector, sem("dve_done"))
    pool = Queue(nc.gpsimd, sem("pool_done"))
    sp = Queue(nc.sync, sem("sp_done"))

    banks = [ctx.enter_context(nc.psum_tensor(f"bank{i}", [P, S], F32)) for i in range(8)]
    free_banks = deque((b, None) for b in banks)

    def take():
        return free_banks.popleft()

    def give(bank, reader):
        free_banks.append((bank, reader))

    ident = sb("ident", [P, P])
    ones = sb("ones", [P, P])
    iota128 = sb("iota128", [P, P])
    iota16 = sb("iota16", [P, TOPK])
    cols = sb("cols", [P, N_COLS])
    window_fix = sb("window_fix", [P, CT, PAD_POOL])
    mod = sb("mod", [P, 48])
    c_act = sb("c_act", [P, KT])
    gain1 = sb("gain1", [P, KT])
    gain2 = sb("gain2", [P, KT])
    subln = sb("subln", [P, 1])

    def col(name, k, w=1):
        base, width = COLS[name]
        assert k + w <= width
        return cols[:, base + k:base + k + w]

    def modc(part, k, w=1):
        return mod[:, part * KT + k:part * KT + k + w]

    x = sb("x", [P, KT, S])
    h_hi = sb("h_hi", [P, KT, S], F32R)
    h_lo = sb("h_lo", [P, KT, S], F32R)
    tmp = sb("tmp", [P, 4, S])
    rstd = sb("rstd", [P, S])
    raw = sb("raw", [P, RAW_SLOTS, SLAB * P])
    w_hi = sb("w_hi", [P, SPLIT_SLOTS, SLAB * P], F32R)
    w_lo = sb("w_lo", [P, SPLIT_SLOTS, SLAB * P], F32R)

    cols_in = counter("cols_in")
    const_in = counter("const_in")
    x_in = counter("x_in")

    cols_ready = act.dma(cols[:], t["cols"], cols_in)
    for dst, name in ((ones, "ones"), (ident, "ident"), (window_fix, "window_fix"), (iota128, "iota128"), (iota16, "iota16")):
        consts_ready = act.dma(dst[:], t[name], const_in)

    tmp_reader = [None] * 4
    tmp_turn = [0]

    def scratch():
        i = tmp_turn[0] % 4
        tmp_turn[0] += 1
        return i, tmp[:, i, :], tmp_reader[i]

    background = []

    def run_background():
        for entry in list(background):
            for _ in range(entry[1]):
                if next(entry[0], "end") == "end":
                    background.remove(entry)
                    break

    def finish(generator):
        for entry in list(background):
            if entry[0] is generator:
                background.remove(entry)
        for _ in generator:
            pass

    order = []

    def plan(name, split=True, slabs=None):
        n = t[name].shape[0]
        order.extend((t[name][i], split) for i in (range(n) if slabs is None else slabs))

    plan("ada_w", split=False, slabs=range(16))
    ada_rest = list(range(16, 48))
    for i in range(t["w_in"].shape[0]):
        plan("w_in", slabs=[i])
        if i < 28:
            plan("ada_w", split=False, slabs=[ada_rest.pop(0)])
    plan("ada_w", split=False, slabs=ada_rest)
    plan("w_merge")
    plan("w_out")
    u_next = 0
    for h in range(HEADS):
        plan("w_query", slabs=[2 * h, 2 * h + 1])
        plan("expert_u", slabs=range(u_next, u_next + UP_PER_HEAD[h]))
        u_next += UP_PER_HEAD[h]
    plan("expert_u", slabs=range(u_next, GELU_SLOTS))
    u_next = GELU_SLOTS
    for g in range(N_GROUPS):
        plan("expert_v", slabs=range(g * KT, (g + 1) * KT))
        for _ in range(GROUP):
            if u_next < EXPERT_TILES:
                plan("expert_u", slabs=[u_next])
                u_next += 1
    plan("ffn1_gate_up")
    plan("ffn1_down")
    plan("w_in_2")
    plan("w_out_2")
    plan("ffn2_gate_up")
    plan("ffn2_down")

    raw_in = [counter(f"raw_in{i}") for i in range(RAW_SLOTS)]
    split_reader = [None] * SPLIT_SLOTS
    landed, parts_ready, split_slot = {}, {}, {}
    raw_done = {}
    n_prepared, n_split, used, used_split = [0], [0], [0], [0]
    lo_engine = [dve]

    def load():
        i = len(landed)
        while i < len(order) and (i < RAW_SLOTS or i - RAW_SLOTS in raw_done):
            landed[i] = sp.dma(raw[:, i % RAW_SLOTS, :], order[i][0], raw_in[i % RAW_SLOTS], raw_done.get(i - RAW_SLOTS))
            i += 1

    def prepare(i):
        if not order[i][1]:
            return
        k = n_split[0] % SPLIT_SLOTS
        n_split[0] += 1
        split_slot[i] = k
        hi, lo, r = w_hi[:, k, :], w_lo[:, k, :], raw[:, i % RAW_SLOTS, :]
        hi_done = act.put(lambda e: e.copy(hi, r), landed[i], split_reader[k])
        raw_done[i] = parts_ready[i] = lo_engine[0].put(lambda e: e.tensor_tensor(lo, r, hi.bitcast(F32), ALU.subtract),
                                               landed[i], hi_done)
        load()

    load()

    def open_slab():
        run_background()
        i = used[0]
        while n_prepared[0] in landed and (n_prepared[0] <= i or n_split[0] <= used_split[0] + SPLIT_AHEAD):
            prepare(n_prepared[0])
            n_prepared[0] += 1
        used[0] += 1
        used_split[0] += order[i][1]
        return i

    def slab_parts(i):
        if order[i][1]:
            return w_hi[:, split_slot[i], :], w_lo[:, split_slot[i], :], parts_ready[i]
        return raw[:, i % RAW_SLOTS, :], None, landed[i]

    def close_slab(i, last):
        if order[i][1]:
            split_reader[split_slot[i]] = last
        else:
            raw_done[i] = last
            load()

    def three(out, a_hi, a_lo, b_hi, b_lo, start, stop, *after):
        pe.put(lambda e: e.matmul(out, a_hi, b_hi, start=start, stop=False), *after, counted=False)
        pe.put(lambda e: e.matmul(out, a_hi, b_lo, start=False, stop=False), counted=False)
        return pe.put(lambda e: e.matmul(out, a_lo, b_hi, start=False, stop=stop))

    cursor = {"slab": None, "block": SLAB}

    def next_block(width=1):
        if cursor["block"] >= SLAB:
            cursor["slab"], cursor["block"] = open_slab(), 0
        i, b = cursor["slab"], cursor["block"]
        cursor["block"] += width
        hi, lo, token = slab_parts(i)
        cut = slice(b * P, (b + width) * P)
        return i, hi[:, cut], None if lo is None else lo[:, cut], token, cursor["block"] >= SLAB

    def project_steps(x_hi, x_lo, kts, x_ready):
        bank, reader = take()
        for j, k in enumerate(kts):
            i, hi, lo, token, last = next_block()
            done = three(bank[:], hi, lo, x_hi[:, k, :], x_lo[:, k, :], j == 0, j == len(kts) - 1,
                         token, reader if j == 0 else None, x_ready[k])
            if last:
                close_slab(i, done)
            yield bank, done

    def project(x_hi, x_lo, kts, x_ready):
        for bank, done in project_steps(x_hi, x_lo, kts, x_ready):
            pass
        return bank, done

    def split(src, hi, lo, *after):
        a = act.put(lambda e: e.copy(hi, src), *after)
        return dve.put(lambda e: e.tensor_tensor(lo, src, hi.bitcast(F32), ALU.subtract), a, *after)

    def feature_sum(tiles, tokens, square=True):
        bank, reader = take()
        for j, (tile, token) in enumerate(zip(tiles, tokens)):
            if square:
                i, sq, r = scratch()
                a = act.put(lambda e, sq=sq, tile=tile: e.activation(sq, tile, ACT.Square), token, r)
                done = pe.put(lambda e, sq=sq, j=j: e.matmul(bank[:], ones[:], sq, start=j == 0, stop=j == len(tiles) - 1),
                              a, reader, consts_ready)
                tmp_reader[i] = done
            else:
                done = pe.put(lambda e, tile=tile, j=j: e.matmul(bank[:], ones[:], tile, start=j == 0, stop=j == len(tiles) - 1),
                              token, reader, consts_ready)
        return bank, done

    rstd_reader = [None]

    def inverse_root(bank, token, width):
        a = dve.put(lambda e: e.tensor_scalar(rstd[:], bank[:], 1.0 / width, EPS, ALU.mult, ALU.add), token, rstd_reader[0])
        give(bank, a)
        b = act.put(lambda e: e.activation(rstd[:], rstd[:], ACT.Sqrt), a)
        return dve.put(lambda e: e.reciprocal(rstd[:], rstd[:]), b)

    def norm_root(x_tok):
        bank, token = feature_sum([x[:, k, :] for k in range(KT)], x_tok)
        return inverse_root(bank, token, D)

    def normed(root, gain, shift, after, h_reader):
        out = []
        for k in range(KT):
            i, s, reader = scratch()
            a = dve.put(lambda e: e.scalar_tensor_tensor(s, x[:, k, :], gain(k), rstd[:], ALU.mult, ALU.mult),
                        root, reader, after)
            rstd_reader[0] = a
            hi, lo = h_hi[:, k, :], h_lo[:, k, :]
            if shift is None:
                b = act.put(lambda e: e.copy(hi, s), a, h_reader)
                done = (pool if k % 3 == 2 else dve).put(lambda e: e.tensor_tensor(lo, s, hi.bitcast(F32), ALU.subtract), b)
            else:
                b = act.put(lambda e: e.activation(hi, s, ACT.Identity, bias=shift(k)), a, h_reader)
                done = dve.put(lambda e: e.scalar_tensor_tensor(lo, s, shift(k), hi.bitcast(F32), ALU.add, ALU.subtract), b)
            tmp_reader[i] = done
            out.append(done)
        return out

    c_ready = act.put(lambda e: e.activation(c_act[:], col("c", 0, 8), ACT.Sigmoid), cols_ready)
    c_ready = dve.put(lambda e: e.tensor_tensor(c_act[:], c_act[:], col("c", 0, 8), ALU.mult), c_ready)
    x_ready = act.dma(x[:], t["x"], x_in)

    mix = ExitStack()
    ada_acc = sb("ada_acc", [P, 2, D], stack=mix)
    x_tok = [x_ready] * KT

    ada = {"n": 0, "token": None, "reader": [None, None], "ready": {}}

    def ada_step():
        part, k = divmod(ada["n"], KT)
        i = open_slab()
        w, _, token = slab_parts(i)
        c = c_act[:, k:k + 1]
        acc = ada_acc[:, part % 2, :]
        if k == 0:
            ada["token"] = dve.put(lambda e: e.tensor_scalar(acc, w, c, None, ALU.mult), token, c_ready, ada["reader"][part % 2])
        else:
            ada["token"] = dve.put(lambda e: e.scalar_tensor_tensor(acc, w, c, acc, ALU.mult, ALU.add), token, ada["token"])
        close_slab(i, ada["token"])
        if k == KT - 1:
            ada["summed"] = (part, ada["token"])
        ada["n"] += 1
        if k == 3 and part > 2:
            ada_sums()

    def ada_sums():
        part, token = ada["summed"]
        acc = ada_acc[:, part % 2, :]
        bank, reader = take()
        for n in range(KT):
            done = pe.put(lambda e: e.matmul(bank[:, n:n + 1], acc[:, n * P:(n + 1) * P], ones[:, 0:1], start=True, stop=True),
                          token, reader, consts_ready)
        ada["reader"][part % 2] = done
        ada["ready"][part] = dve.put(lambda e: e.tensor_tensor(
            mod[:, part * KT:(part + 1) * KT], bank[:, 0:KT], col("ada_b", part * KT, KT), ALU.add), done, consts_ready)
        give(bank, ada["ready"][part])

    for _ in range(KT):
        ada_step()
    ada_sums()
    root = norm_root(x_tok)
    for _ in range(KT):
        ada_step()
    ada_sums()
    gain1_ready = dve.put(lambda e: e.scalar_tensor_tensor(gain1[:], modc(1, 0, KT), 1.0, col("norm1_g", 0, KT), ALU.add, ALU.mult),
                          ada["ready"][1])
    h_ready = normed(root, lambda k: gain1[:, k:k + 1], lambda k: modc(0, k), [x_ready, gain1_ready], None)

    gates = sb("gates", [P, 2 * KT, S], stack=mix)
    conv = sb("conv", [P, CT, S], stack=mix)
    mixed = sb("mixed", [P, CT, S], stack=mix)
    pool_w = sb("pool_w", [P, CT, P], stack=mix)
    front = ExitStack()
    p_pad = sb("p_pad", [P, CT, PAD_POOL + S], stack=front)
    a_val = sb("a_val", [P, S], stack=front)
    glu = sb("glu", [P, CT, PAD_CONV + S], stack=front)
    pooled = sb("pooled", [P, 2, PAD_POOL + S], stack=front)
    prod = sb("prod", [P, 2, 2, S], stack=front)

    pads = pool.put(lambda e: e.memset(p_pad[:, :, 0:PAD_POOL], 0.0))
    pads = pool.put(lambda e: e.memset(glu[:, :, 0:PAD_CONV], 0.0))

    def interleave_ada():
        if ada["n"] < 44:
            ada_step()

    p_ready = []
    for c in range(CT):
        bank, token = project(h_hi, h_lo, range(KT), h_ready)
        interleave_ada()
        a = act.put(lambda e, bank=bank, c=c: e.activation(p_pad[:, c, PAD_POOL:], bank[:], ACT.Identity, bias=col("b_in", c)), token)
        give(bank, a)
        p_ready.append(a)

    mixed_ready = []
    pool_prev = None
    for c, w in enumerate(POOL_WINDOWS):
        src, token, shift, lv = p_pad[:, c, :], [p_ready[c], pads, pool_prev], 1, 0
        lo_col = 0
        while shift < w:
            lo_col += shift
            dst = pooled[:, lv % 2, :]
            token = pool.put(lambda e, dst=dst, src=src, shift=shift, lo_col=lo_col: e.tensor_tensor(
                dst[:, lo_col:], src[:, lo_col:], src[:, lo_col - shift:PAD_POOL + S - shift], ALU.add), token)
            src, shift, lv = dst, shift * 2, lv + 1
        body = mixed[:, c, :]
        a = pool.put(lambda e, body=body, src=src, w=w: e.tensor_scalar(body, src[:, PAD_POOL:], 1.0 / w, None, ALU.mult), token)
        a = pool.put(lambda e, body=body, c=c: e.tensor_tensor(body[:, 0:PAD_POOL], body[:, 0:PAD_POOL], window_fix[:, c, :], ALU.mult),
                     a, consts_ready)
        pool_prev = pool.put(lambda e, body=body, c=c: e.tensor_tensor(body, body, p_pad[:, c, PAD_POOL:], ALU.subtract), a)
        mixed_ready.append(pool_prev)

    glu_ready = []
    a_val_reader = None
    for c in range(CT):
        bank, token = project(h_hi, h_lo, range(KT), h_ready)
        interleave_ada()
        a = act.put(lambda e, bank=bank, c=c: e.activation(a_val[:], bank[:], ACT.Identity, bias=col("b_in", CT + c)),
                    token, a_val_reader)
        give(bank, a)
        bank, token = project(h_hi, h_lo, range(KT), h_ready)
        interleave_ada()
        i, s, r = scratch()
        b = act.put(lambda e, bank=bank, s=s, c=c: e.activation(s, bank[:], ACT.Sigmoid, bias=col("b_in", 2 * CT + c)), token, r)
        give(bank, b)
        a_val_reader = dve.put(lambda e, s=s, c=c: e.tensor_tensor(glu[:, c, PAD_CONV:], a_val[:], s, ALU.mult), b, a)
        tmp_reader[i] = a_val_reader
        glu_ready.append(a_val_reader)

    conv_token = [None] * CT
    prod_reader = [[None, None], [None, None], [None, None], [None, None]]

    def convolve():
        for j in range(CONV_K):
            for c in range(CT):
                tap = col("dw_kernel", c * CONV_K + j)
                src = glu[:, c, j:j + S]
                acc = conv[:, c, :]
                if c < 2 and j == 0:
                    conv_token[c] = dve.put(lambda e: e.tensor_scalar(acc, src, tap, col("dw_bias", c), ALU.mult, ALU.add),
                                            glu_ready[c], pads)
                elif c < 2:
                    conv_token[c] = dve.put(lambda e: e.scalar_tensor_tensor(acc, src, tap, acc, ALU.mult, ALU.add), conv_token[c])
                elif j == 0:
                    conv_token[c] = act.put(lambda e: e.activation(acc, src, ACT.Identity, scale=tap, bias=col("dw_bias", c)),
                                            glu_ready[c], pads)
                else:
                    one = prod[:, c - 2, j % 2, :]
                    a = act.put(lambda e: e.activation(one, src, ACT.Copy, scale=tap), glu_ready[c], pads, prod_reader[c][j % 2])
                    conv_token[c] = prod_reader[c][j % 2] = pool.put(lambda e: e.tensor_tensor(acc, acc, one, ALU.add),
                                                                     a, conv_token[c])
                if c % 2:
                    yield

    front_done = []

    def branches():
        for _ in convolve():
            yield
        front_done.extend(conv_token + [pool_prev])
        bank, token = feature_sum([conv[:, c, :] for c in range(CT)], conv_token, square=False)
        yield
        yield
        for c in range(CT):
            a = dve.put(lambda e: e.scalar_tensor_tensor(conv[:, c, :], bank[:], -1.0 / CW, conv[:, c, :], ALU.mult, ALU.add), token)
            conv_token[c] = a
        give(bank, a)
        yield
        for c in range(CT):
            bank_g, reader = take()
            a = pe.put(lambda e: e.matmul(bank_g[:], pool_w[:, c, :], mixed[:, c, :], start=True, stop=True),
                       mixed_ready[c], pool_w_ready, reader)
            i, s, r = scratch()
            a = dve.put(lambda e: e.tensor_scalar(s, bank_g[:], col("pool_scale", c), None, ALU.mult), a, r)
            give(bank_g, a)
            b_ready[c] = tmp_reader[i] = split(s, b_hi[:, c, :], b_lo[:, c, :], a, front_done)
            yield
        bank, token = feature_sum([conv[:, c, :] for c in range(CT)], conv_token)
        yield
        yield
        root = inverse_root(bank, token, CW)
        yield
        for c in range(CT):
            a = dve.put(lambda e: e.scalar_tensor_tensor(conv[:, c, :], conv[:, c, :], col("conv_ln_g", c), rstd[:], ALU.mult, ALU.mult), root)
            rstd_reader[0] = a
            i, s, rd = scratch()
            b = act.put(lambda e: e.activation(s, conv[:, c, :], ACT.Sigmoid, bias=col("conv_ln_b", c)), a, rd)
            b = dve.put(lambda e: e.scalar_tensor_tensor(s, conv[:, c, :], col("conv_ln_b", c), s, ALU.add, ALU.mult), b)
            b_ready[CT + c] = tmp_reader[i] = split(s, b_hi[:, CT + c, :], b_lo[:, CT + c, :], b, front_done)
            yield

    pool_w_in = counter("pool_w_in")
    pool_w_ready = act.dma(pool_w[:], t["pool_w"], pool_w_in)
    front.close()
    b_hi = sb("b_hi", [P, KT, S], F32R, stack=mix)
    b_lo = sb("b_lo", [P, KT, S], F32R, stack=mix)
    b_ready = [None] * KT
    branch_work = branches()
    background.append([branch_work, 2])

    gate_ready = []
    for n in range(2 * KT):
        bank, token = project(h_hi, h_lo, range(KT), h_ready)
        interleave_ada()
        a = act.put(lambda e, bank=bank, n=n: e.activation(gates[:, n, :], bank[:], ACT.Sigmoid, bias=col("b_in", 3 * CT + n)), token)
        give(bank, a)
        gate_ready.append(a)
    while ada["n"] < 48:
        ada_step()
    ada_sums()
    finish(branch_work)
    h_reader = token

    merged_ready = []
    for n in range(KT):
        bank_p, token_p = project(b_hi, b_lo, range(CT), b_ready)
        bank_c, token_c = project(b_hi, b_lo, range(CT, KT), b_ready)
        i, s, r = scratch()
        a = dve.put(lambda e, s=s, n=n, bank=bank_p: e.tensor_tensor(s, bank[:], gates[:, n, :], ALU.mult), token_p, r, gate_ready[n])
        give(bank_p, a)
        i2, s2, r2 = scratch()
        b = dve.put(lambda e, s2=s2, n=n, bank=bank_c: e.tensor_tensor(s2, bank[:], gates[:, KT + n, :], ALU.mult), token_c, r2, gate_ready[KT + n])
        give(bank_c, b)
        c_ = pool.put(lambda e, s=s, s2=s2: e.tensor_tensor(s, s, s2, ALU.add), a, b)
        tmp_reader[i2] = c_
        done = split(s, h_hi[:, n, :], h_lo[:, n, :], c_, h_reader)
        tmp_reader[i] = done
        merged_ready.append(done)

    for n in range(KT):
        bank, token = project(h_hi, h_lo, range(KT), merged_ready)
        a = dve.put(lambda e, bank=bank, n=n: e.scalar_tensor_tensor(x[:, n, :], bank[:], modc(2, n), x[:, n, :], ALU.mult, ALU.add), token)
        give(bank, a)
        x_tok[n] = a
    mix_done = [token, a, pool_prev, act.put(lambda e: e.copy(gain2[:], gain1[:]))]
    mix.close()

    gain2_ready = dve.put(lambda e: e.scalar_tensor_tensor(gain2[:], modc(4, 0, KT), 1.0, col("norm2_g", 0, KT), ALU.add, ALU.mult),
                          mix_done)
    h_ready = normed(norm_root(x_tok), lambda k: gain2[:, k:k + 1], lambda k: modc(3, k), gain2_ready, token)

    peer = ExitStack()
    gelu = sb("gelu", [P, GELU_SLOTS, S], stack=peer)
    staging = ExitStack()
    sel_s = sb("sel_s", [P, TT, HEADS, TOPK], stack=staging)
    sel_i = sb("sel_i", [P, 2, TT, HEADS, TOPK], stack=staging)
    soft = sb("soft", [P, TT * HEADS], stack=staging)
    sel_t = sb("sel_t", [P, 3, S], stack=staging)
    neg_t = sb("neg_t", [P, 2, S], stack=staging)
    hot2 = sb("hot2", [P, HOT_SLOTS, TOK4, P], stack=staging)
    hot1 = sb("hot1", [P, HOT_SLOTS, TOK4, P], stack=staging)
    choosing = ExitStack()
    keys = sb("keys", [P, 2, P], stack=choosing)
    q_t = sb("q_t", [P, 2, S], stack=choosing)
    top = sb("top", [P, TT, 2, TOPK], stack=choosing)
    top_u = sb("top_u", [P, TT, 2, TOPK], U32, stack=choosing)
    top_f = sb("top_f", [P, TT, 2, TOPK], stack=choosing)
    rest = sb("rest", [P, TT, 2 * P], stack=choosing)
    cand = sb("cand", [P, TT, TOPK, TOPK], stack=choosing)
    pos = sb("pos", [P, TT, TOPK], U32, stack=choosing)
    pos_u = sb("pos_u", [P, 2, TT, TOPK], U32, stack=choosing)
    pos_f = sb("pos_f", [P, 2, TT, TOPK], stack=choosing)
    keys_in = counter("keys_in")
    keys_ready = act.dma(keys[:], t["keys"], keys_in, *mix_done)

    routed = []

    q_reader = [None]

    def best_sixteen(scores, values, places, n, after):
        tiles = range(TT)
        first = [dve.put(lambda e: e.max(values[i][:, 0:8], scores[i]), *after) for i in tiles]
        yield
        left = [dve.put(lambda e: e.match_replace(rest[:, i, 0:n], values[i][:, 0:8], scores[i], NEG), first[i]) for i in tiles]
        yield
        for i in tiles:
            dve.put(lambda e: e.max_index(places[i][:, 0:8], values[i][:, 0:8], scores[i]), first[i])
        yield
        second = [dve.put(lambda e: e.max(values[i][:, 8:16], rest[:, i, 0:n]), left[i]) for i in tiles]
        yield
        for i in tiles:
            dve.put(lambda e: e.max_index(places[i][:, 8:16], values[i][:, 8:16], rest[:, i, 0:n]), second[i])
        yield

    def route(h):
        bank_of = []
        for half in range(2):
            bank, reader = take()
            for tt in range(TT):
                a = pe.put(lambda e, bank=bank, half=half, tt=tt: e.matmul(
                    bank[:, tt * P:(tt + 1) * P], q_t[:, half, tt * P:(tt + 1) * P], keys[:, half, :], start=True, stop=True),
                    q_ready[half], reader, keys_ready, mix_done)
            bank_of.append((bank, a))
        q_reader[0] = a
        last = None
        for half in range(2):
            bank, token = bank_of[half]
            s = [bank[:, tt * P:(tt + 1) * P] for tt in range(TT)]
            for step in best_sixteen(s, [top[:, tt, half, :] for tt in range(TT)], [top_u[:, tt, half, :] for tt in range(TT)],
                                     P, [token, routed[-1:] or mix_done]):
                yield
            last = (dve, dve.count)
            give(bank, last)
        top_ready = dve.put(lambda e: e.tensor_copy(top_f[:], top_u[:]), last)
        one = top[:, :, 0, :].unsqueeze(3).to_broadcast([P, TT, TOPK, TOPK])
        two = top[:, :, 1, :].unsqueeze(2).to_broadcast([P, TT, TOPK, TOPK])
        cand_ready = pool.put(lambda e: e.tensor_tensor(cand[:], one, two, ALU.add), last)
        yield
        for step in best_sixteen([cand[:, tt, :, :].rearrange("p a b -> p (a b)") for tt in range(TT)],
                                 [sel_s[:, tt, h, :] for tt in range(TT)], [pos[:, tt, :] for tt in range(TT)], 2 * P, [cand_ready]):
            yield
        last = (dve, dve.count)
        a = dve.put(lambda e: e.tensor_single_scalar(pos_u[:, 0], pos[:], 4, ALU.logical_shift_right), last)
        b = dve.put(lambda e: e.tensor_single_scalar(pos_u[:, 1], pos[:], TOPK - 1, ALU.bitwise_and), last)
        pos_ready = dve.put(lambda e: e.tensor_copy(pos_f[:], pos_u[:]), b)
        yield
        iota_b = iota16[:].unsqueeze(1).unsqueeze(1).to_broadcast([P, TT, TOPK, TOPK])
        for half in range(2):
            pf = pos_f[:, half].unsqueeze(3).to_broadcast([P, TT, TOPK, TOPK])
            tf = top_f[:, :, half, :].unsqueeze(2).to_broadcast([P, TT, TOPK, TOPK])
            a = dve.put(lambda e, pf=pf: e.tensor_tensor(cand[:], pf, iota_b, ALU.is_equal), pos_ready, consts_ready, top_ready, last)
            a = pool.put(lambda e, tf=tf: e.tensor_tensor(cand[:], cand[:], tf, ALU.mult), a)
            last = dve.put(lambda e, half=half: e.tensor_reduce(sel_i[:, half, :, h, :], cand[:], AX_X, ALU.add), a)
            yield
        routed.append(last)

    gelu_reader = [mix_done] * GELU_SLOTS
    gelu_ready = {}

    def expert_up_steps(b):
        for bank, token in project_steps(h_hi, h_lo, range(KT), h_ready):
            yield
        s = b % GELU_SLOTS
        gelu_ready[b] = act.put(lambda e, bank=bank, s=s: e.activation(gelu[:, s, :], bank[:], ACT.Gelu_apprx_tanh), token, gelu_reader[s])
        give(bank, gelu_ready[b])

    def expert_up(b):
        for _ in expert_up_steps(b):
            pass

    lo_engine[0] = pool
    route_work = []
    for h in range(HEADS):
        q_ready = []
        for half in range(2):
            bank, token = project(h_hi, h_lo, range(KT), h_ready)
            a = act.put(lambda e, bank=bank, half=half: e.copy(q_t[:, half, :], bank[:]), token, q_reader[0], mix_done)
            give(bank, a)
            q_ready.append(a)
        if route_work:
            finish(route_work[-1])
        work = route(h)
        route_work.append(work)
        next(work)
        background.append([work, 5])
        for _ in range(UP_PER_HEAD[h]):
            expert_up(len(gelu_ready))

    g_dram = t["g_scratch"]
    chunk_out = [counter("chunk_out0"), counter("chunk_out1")]
    chunk_out_done = [None, None]

    def routing_matrix():
        v = sel_s[:].rearrange("p t h k -> p (t h) k")
        best = sel_s[:, :, :, 0:1].rearrange("p t h k -> p (t h) k").to_broadcast([P, TT * HEADS, TOPK])
        e_ = cand[:].rearrange("p t a b -> p (t a b)")[:, 0:TT * HEADS * TOPK].rearrange("p (g k) -> p g k", k=TOPK)
        a = dve.put(lambda e: e.tensor_tensor(e_, v, best, ALU.subtract), routed[-1])
        a = act.put(lambda e: e.activation(e_, e_, ACT.Exp), a)
        b = dve.put(lambda e: e.tensor_reduce(soft[:], e_, AX_X, ALU.add), a)
        b = dve.put(lambda e: e.reciprocal(soft[:], soft[:]), b)
        gate = dve.put(lambda e: e.tensor_tensor(v, e_, soft[:].unsqueeze(2).to_broadcast([P, TT * HEADS, TOPK]), ALU.mult), b)
        stage_free = [gate, q_reader[0]]
        choosing.close()
        stage_all = sb("stage", [P, 2, P, CHUNK], stack=staging)
        yield
        sel_ready = []
        for n, src in enumerate((sel_s[:], sel_i[:, 0], sel_i[:, 1])):
            bank, reader = take()
            for tt in range(TT):
                a = pe.put(lambda e, bank=bank, tt=tt, src=src: e.transpose(
                    bank[:, tt * P:(tt + 1) * P], src[:, tt].rearrange("p h k -> p (h k)"), ident[:]), gate, reader, consts_ready)
            a = act.put(lambda e, bank=bank, n=n: e.copy(sel_t[:, n, :], bank[:]), a)
            give(bank, a)
            sel_ready.append(a)
            if n < 2:
                sel_ready.append(act.put(lambda e: e.mul(neg_t[:, n, :], sel_t[:, n, :], -1.0), a))
        yield
        hot_reader = [None] * HOT_SLOTS
        hot_ready, summed = {}, {}

        def one_hots(g):
            r, t0 = g % HOT_SLOTS, g * TOK4
            key2 = sel_t[:, 2, t0:t0 + TOK4].unsqueeze(2).to_broadcast([P, TOK4, P])
            hot_ready[g] = [dve.put(lambda e: e.tensor_tensor(
                hot2[:, r], iota128[:].unsqueeze(1).to_broadcast([P, TOK4, P]), key2, ALU.is_equal), sel_ready, hot_reader[r])]
            for j in range(TOK4):
                one, key1, gate1 = hot1[:, r, j, :], sel_t[:, 1, t0 + j:t0 + j + 1], sel_t[:, 0, t0 + j:t0 + j + 1]
                if j == 3:
                    b = act.put(lambda e: e.activation(one, iota128[:], ACT.Abs, bias=neg_t[:, 1, t0 + j:t0 + j + 1]),
                                sel_ready, hot_reader[r])
                    b = act.put(lambda e: e.activation(one, one, ACT.Relu, bias=gate1, scale=neg_t[:, 0, t0 + j:t0 + j + 1]), b)
                else:
                    b = (pool if j == 0 else dve).put(lambda e: e.tensor_scalar(one, iota128[:], key1, gate1, ALU.is_equal, ALU.mult),
                                                      sel_ready, hot_reader[r])
                hot_ready[g].append(b)

        def routing_products(g):
            r = g % HOT_SLOTS
            bank, reader = take()
            for j in range(TOK4):
                c = pe.put(lambda e: e.matmul(bank[:, j * P:(j + 1) * P], hot2[:, r, j, :], hot1[:, r, j, :], start=True, stop=True),
                           hot_ready[g], reader)
            hot_reader[r] = c
            summed[g] = (bank, c)

        def to_chunk(g):
            t0 = g * TOK4
            o, half = t0 % CHUNK, t0 // CHUNK % 2
            bank, c = summed.pop(g)
            done = act.put(lambda e: e.copy(
                stage_all[:, half, :, o:o + TOK4].rearrange("p b t -> p t b"), bank[:].rearrange("p (t b) -> p t b", t=TOK4)),
                c, chunk_out_done[half], stage_free)
            give(bank, done)
            if o + TOK4 == CHUNK:
                chunk_out_done[half] = act.dma(g_dram[t0 // CHUNK], stage_all[:, half], chunk_out[half], done)

        groups = S // TOK4
        for step in range(groups + 2):
            if step < groups:
                one_hots(step)
            if 0 <= step - 1 < groups:
                routing_products(step - 1)
            if step >= 2:
                to_chunk(step - 2)
            yield
        g_written.extend(chunk_out_done)

    g_written = []
    matrix_work = routing_matrix()
    finish(route_work[-1])
    up_work = (None for b in range(len(gelu_ready), GELU_SLOTS) for _ in expert_up_steps(b))
    for step, _ in enumerate(matrix_work):
        if step % UP_EVERY == 0:
            next(up_work, None)
    for _ in up_work:
        pass
    lo_engine[0] = dve

    staging.close()
    g_tile = sb("g_tile", [P, G_SLOTS, S // CHUNK, G_TILES, CHUNK], stack=peer)
    act_hi = sb("act_hi", [P, GROUP, S], F32R, stack=peer)
    act_lo = sb("act_lo", [P, GROUP, S], F32R, stack=peer)
    g_in = [counter(f"g_in{i}") for i in range(G_SLOTS)]
    g_reader = [g_written] * G_SLOTS
    g_landed = {}
    w_ready = {}
    v_last = [None]

    def load_g(n):
        if n * G_TILES < EXPERT_TILES:
            s = n % G_SLOTS
            g_landed[n] = sp.dma(g_tile[:, s].rearrange("p c b t -> p c (b t)"),
                                 g_dram[:, :, n * G_TILES:(n + 1) * G_TILES, :].rearrange("c p b t -> p c (b t)"),
                                 g_in[s], g_written, g_reader[s])

    def weigh(b):
        s, n = b % GELU_SLOTS, b // G_TILES
        src = gelu[:, s, :]
        g_b = g_tile[:, n % G_SLOTS, :, b % G_TILES, :]
        a = dve.put(lambda e: e.tensor_tensor(src.rearrange("p (c t) -> p c t", t=CHUNK), src.rearrange("p (c t) -> p c t", t=CHUNK),
                                              g_b, ALU.mult), gelu_ready[b], g_landed[n])
        if b % G_TILES == G_TILES - 1:
            g_reader[n % G_SLOTS] = a
            load_g(n + G_SLOTS)
        k = b % GROUP
        w_ready[b] = gelu_reader[s] = split(src, act_hi[:, k, :], act_lo[:, k, :], a, v_last[0], g_written)

    for n in range(G_SLOTS):
        load_g(n)
    for b in range(GROUP):
        weigh(b)
    u_next = GELU_SLOTS
    for g in range(N_GROUPS):
        ready_w = [w_ready[g * GROUP + j] for j in range(GROUP)]
        for dt in range(KT):
            bank, token = project(act_hi, act_lo, range(GROUP), ready_w)
            x_tok[dt] = dve.put(lambda e, bank=bank, dt=dt: e.scalar_tensor_tensor(
                x[:, dt, :], bank[:], modc(5, dt), x[:, dt, :], ALU.mult, ALU.add), token, x_tok[dt])
            give(bank, x_tok[dt])
        v_last[0] = token
        for j in range(GROUP):
            if u_next < EXPERT_TILES:
                expert_up(u_next)
                u_next += 1
            if g + 1 < N_GROUPS:
                weigh((g + 1) * GROUP + j)
    peer_done = [token, (act, act.count), (dve, dve.count), (pool, pool.count)]
    peer.close()

    def norm_in_place(name, x_tok):
        root = norm_root(x_tok)
        for k in range(KT):
            x_tok[k] = rstd_reader[0] = dve.put(lambda e: e.scalar_tensor_tensor(
                x[:, k, :], x[:, k, :], col(name, k), rstd[:], ALU.mult, ALU.mult), root)

    norm_in_place("final_g", x_tok)

    def swiglu(norm_name, place_free, h_reader):
        hr = normed(norm_root(x_tok), lambda k: col(norm_name, k), None, None, h_reader)
        with ExitStack() as ffn:
            f_hi = sb(norm_name + "_f_hi", [P, FT, S], F32R, stack=ffn)
            f_lo = sb(norm_name + "_f_lo", [P, FT, S], F32R, stack=ffn)
            f_ready = []
            for n in range(FT):
                bank_g, token_g = project(h_hi, h_lo, range(KT), hr)
                bank_u, token_u = project(h_hi, h_lo, range(KT), hr)
                i, s, r = scratch()
                a = act.put(lambda e, s=s, bank=bank_g: e.activation(s, bank[:], ACT.Silu), token_g, r)
                give(bank_g, a)
                b = dve.put(lambda e, s=s, bank=bank_u: e.tensor_tensor(s, s, bank[:], ALU.mult), token_u, a)
                give(bank_u, b)
                tmp_reader[i] = split(s, f_hi[:, n, :], f_lo[:, n, :], b, place_free)
                f_ready.append(tmp_reader[i])
            for n in range(KT):
                bank, token = project(f_hi, f_lo, range(FT), f_ready)
                a = dve.put(lambda e, bank=bank, n=n: e.scalar_tensor_tensor(x[:, n, :], bank[:], 0.5, x[:, n, :], ALU.mult, ALU.add), token)
                give(bank, a)
                x_tok[n] = a
        return token_u, token

    h_reader, f_reader = swiglu("ffn1_norm_2", peer_done, peer_done[0])

    att = ExitStack()
    qk_t = sb("qk_t", [P, 16, S], stack=att)
    v_nat = sb("v_nat", [P, TT, D], stack=att)
    bias = sb("bias", [P, 4, S], stack=att)
    mult = sb("mult", [P, S], stack=att)
    lam_in = sb("lam_in", [P, 4, DH], stack=att)
    lam = sb("lam", [P, 8], stack=att)
    stat = sb("stat", [P, 2 * TT * N_MAPS], stack=att)
    tables = ExitStack()
    table = sb("table", [DH, N_MAPS], stack=tables)
    buckets = sb("buckets", [DH, 2, BIAS_L], stack=tables)
    by_dist = sb("by_dist", [DIL_HEADS, 2, BIAS_L], stack=tables)
    att_in = counter("att_in")
    bias_out = counter("bias_out")
    bias_in = [counter(f"bias_in{i}") for i in range(4)]

    old = [f_reader, (act, act.count)]
    for dst, name in ((table, "rel_bias"), (buckets, "buckets"), (mult, "mult"), (lam_in, "lam_in")):
        att_ready = sp.dma(dst[:], t[name], att_in, *old)
    bank_pair = [take(), take()]
    for m, (width, off) in enumerate(((S, 0), (BIAS_L - S, S))):
        for kind in range(2):
            bank, reader = (take() if (m, kind) != (0, 0) else bank_pair[0])
            a = pe.put(lambda e, bank=bank, kind=kind, off=off, width=width: e.matmul(
                bank[0:DIL_HEADS, 0:width], table[:, kind * 8:kind * 8 + 8], buckets[:, kind, off:off + width],
                start=True, stop=True), att_ready, reader)
            a = act.put(lambda e, bank=bank, kind=kind, off=off, width=width: e.mul(
                by_dist[:, kind, off:off + width], bank[0:DIL_HEADS, 0:width], DH ** 0.5), a)
            give(bank, a)
    free_banks.append(bank_pair[1])
    b_dram = t["bias_scratch"]
    for kind in range(2):
        b_out = act.dma(b_dram[:, kind * 8:kind * 8 + 8, :].rearrange("q m x -> m q x"),
                        by_dist[:, kind, :].unsqueeze(1).to_broadcast([DIL_HEADS, P, BIAS_L]), bias_out, a)
    bias_reader = [old] * 4
    bias_ready = {}

    def load_bias(m):
        if m < N_MAPS:
            skew = bass.AP(b_dram.tensor, m * BIAS_L + P - 1, [[N_MAPS * BIAS_L - 1, P], [1, S]])
            bias_ready[m] = pool.dma(bias[:, m % 4, :], skew, bias_in[m % 4], b_out, bias_reader[m % 4])

    for m in range(4):
        load_bias(m)
    tables.close()

    a = dve.put(lambda e: e.tensor_tensor(lam_in[:, 0:2, :], lam_in[:, 0:2, :], lam_in[:, 2:4, :], ALU.mult), att_ready)
    a = dve.put(lambda e: e.tensor_reduce(lam[:, 0:2], lam_in[:, 0:2, :], AX_X, ALU.add), a)
    a = act.put(lambda e: e.activation(lam[:, 2:4], lam[:, 0:2], ACT.Exp), a)
    a = dve.put(lambda e: e.tensor_tensor(lam[:, 4:5], lam[:, 2:3], lam[:, 3:4], ALU.subtract), a)
    a = dve.put(lambda e: e.tensor_scalar(lam[:, 5:6], lam[:, 4:5], LAM0, None, ALU.add), a)
    lam_ready = dve.put(lambda e: e.tensor_scalar(subln[:], col("subln_gain_2", 0), 1.0 - LAM0, None, ALU.mult), a)

    h_ready = normed(norm_root(x_tok), lambda k: col("mix_norm_2", k), None, None, h_reader)
    qk_ready = [None] * 16
    for n in range(16):
        bank, token = project(h_hi, h_lo, range(KT), h_ready)
        qk_ready[n] = act.put(lambda e, bank=bank, n=n: e.copy(qk_t[:, n, :], bank[:]), token, old)
        give(bank, qk_ready[n])
    v_ready = None
    for half in range(2):
        four = [take() for _ in range(TT)]
        for k in range(KT):
            i, w_h, w_l, token, last = next_block(4)
            for tt in range(TT):
                cut = slice(tt * P, (tt + 1) * P)
                done = three(four[tt][0][:], h_hi[:, k, cut], h_lo[:, k, cut], w_h, w_l, k == 0, k == KT - 1,
                             token, four[tt][1] if k == 0 else None, h_ready[k])
            if last:
                close_slab(i, done)
        for tt in range(TT):
            v_ready = act.put(lambda e, bank=four[tt][0], tt=tt, half=half: e.copy(v_nat[:, tt, half * S:(half + 1) * S], bank[:]), done, old)
            give(four[tt][0], v_ready)
    h_reader = done

    maps = [(c, 4 + c, DH * m, 2 * c + m) for c in range(DIFF_HEADS) for m in range(2)]
    maps += [(8 + h // 2, 12 + h // 2, DH * (h % 2), 8 + h) for h in range(DIL_HEADS)]
    probs_turn = [0]
    probs_reader = [None, None]
    prob_t_reader = [None]
    stat_n = [0]

    probs = sb("probs", [P, 3, 2, S], stack=att)
    prob_t = sb("prob_t", [P, 2, TT, S], stack=att)
    place_free = [b_out]
    probs_reader = [None] * 3
    prob_t_reader = [None] * 2
    b_ready = [None] * KT

    def scores(unit):
        slot, width = unit["n"] % 3, (unit["qt"] + 1) * P
        unit["maps_done"] = []
        for m, mid in enumerate(unit["maps"]):
            qi, ki, off, bc = maps[mid]
            rows, cols_q = slice(off, off + DH), slice(width - P, width)
            bank, reader = take()
            a = pe.put(lambda e: e.matmul(bank[:, 0:width], qk_t[rows, qi, cols_q], qk_t[rows, ki, 0:width], start=True, stop=True),
                       qk_ready[qi], qk_ready[ki], reader)
            w = probs[:, slot, m, 0:width]
            k = 2 * (mid * TT + unit["qt"])
            top_c, sum_c = stat[:, k:k + 1], stat[:, k + 1:k + 2]
            a = dve.put(lambda e: e.tensor_tensor_reduce(out=w, in0=bank[:, 0:width], in1=bias[:, bc % 4, S - width:S], scale=DH ** -0.5,
                                                         scalar=-3.0e38, op0=ALU.add, op1=ALU.max, accum_out=top_c),
                        a, bias_ready[bc], probs_reader[slot], old, place_free)
            give(bank, a)
            bias_reader[bc % 4] = a
            if unit["qt"] == TT - 1:
                load_bias(bc + 4)
            b = dve.put(lambda e: e.tensor_scalar(top_c, top_c, -1.0, None, ALU.mult), a)
            if unit["diff"]:
                b = act.put(lambda e: e.activation(w, w, ACT.Exp, bias=top_c, accum_out=sum_c), b)
            else:
                b = act.put(lambda e: e.activation(w, w, ACT.Exp, bias=top_c), b)
            unit["maps_done"].append((w, sum_c, b))

    def weights(unit):
        width = (unit["qt"] + 1) * P
        done = []
        for m, (w, sum_c, b) in enumerate(unit["maps_done"]):
            if not unit["diff"]:
                b = dve.put(lambda e: e.tensor_tensor_reduce(out=w, in0=w, in1=mult[:, S - width:S], scale=1.0, scalar=0.0,
                                                             op0=ALU.mult, op1=ALU.add, accum_out=sum_c), b, att_ready)
            b = dve.put(lambda e: e.reciprocal(sum_c, sum_c), b)
            done.append((w, sum_c, b))
        w0, s0, b0 = done[0]
        if unit["diff"]:
            w1, s1, b1 = done[1]
            b1 = dve.put(lambda e: e.tensor_tensor(s1, s1, lam[:, 5:6], ALU.mult), b1, lam_ready)
            b0 = dve.put(lambda e: e.tensor_scalar(w0, w0, s0, None, ALU.mult), b0)
            unit["w"] = dve.put(lambda e: e.scalar_tensor_tensor(w0, w1, s1, w0, ALU.mult, ALU.subtract, reverse1=True), b1, b0)
        else:
            unit["w"] = dve.put(lambda e: e.tensor_scalar(w0, w0, s0, None, ALU.mult), b0)

    def turn(unit):
        slot, qt = unit["n"] % 3, unit["qt"]
        bank, reader = take()
        for kt in range(qt + 1):
            a = pe.put(lambda e: e.transpose(bank[:, kt * P:(kt + 1) * P], probs[:, slot, 0, kt * P:(kt + 1) * P], ident[:]),
                       unit["w"], reader)
        probs_reader[slot] = a
        k = unit["head"] % 2
        a = act.put(lambda e: e.copy(prob_t[:, k, 0:qt + 1, qt * P:(qt + 1) * P],
                                     bank[:, 0:(qt + 1) * P].rearrange("p (k q) -> p k q", q=P)), a, prob_t_reader[k], place_free)
        give(bank, a)
        return a

    pair_bank = {}

    def weigh_values(unit, ready_t):
        head, k = unit["head"], unit["head"] % 2
        if unit["diff"]:
            bank, reader = take()
            rows, v_cols = slice(0, P), slice(head * P, (head + 1) * P)
        else:
            h = head - DIFF_HEADS
            if h % 2 == 0:
                pair_bank["bank"] = take()
            bank, reader = pair_bank["bank"]
            rows, v_cols = slice(DH * (h % 2), DH * (h % 2 + 1)), slice(S + h * DH, S + (h + 1) * DH)
        for kt in range(TT):
            a = pe.put(lambda e: e.matmul(bank[rows, kt * P:], v_nat[:, kt, v_cols], prob_t[:, k, kt, kt * P:], start=kt == 0, stop=kt == TT - 1),
                       ready_t, v_ready, reader)
        prob_t_reader[k] = a
        if unit["diff"]:
            oa_ready.append(act.put(lambda e: e.copy(qk_t[:, head, :], bank[:]), a))
            give(bank, oa_ready[-1])
        elif h % 2:
            c = DIFF_HEADS + h // 2
            i, s, r = scratch()
            a = act.put(lambda e: e.copy(s, bank[:]), a, r)
            give(bank, a)
            b_ready[c] = tmp_reader[i] = split(s, h_hi[:, c, :], h_lo[:, c, :], a, h_reader)

    oa_ready = []

    def diff_norm():
        roots = []
        for c in range(DIFF_HEADS):
            bank, token = feature_sum([qk_t[:, c, :]], [oa_ready[c]])
            yield
            a = dve.put(lambda e: e.tensor_scalar(qk_t[:, DIFF_HEADS + c, :], bank[:], 1.0 / P, EPS, ALU.mult, ALU.add), token)
            give(bank, a)
        a = act.put(lambda e: e.activation(qk_t[:, DIFF_HEADS:2 * DIFF_HEADS, :], qk_t[:, DIFF_HEADS:2 * DIFF_HEADS, :], ACT.Sqrt), a)
        yield
        yield
        for c in range(DIFF_HEADS):
            b = dve.put(lambda e: e.reciprocal(qk_t[:, DIFF_HEADS + c, :], qk_t[:, DIFF_HEADS + c, :]), a)
            yield
            b = dve.put(lambda e: e.scalar_tensor_tensor(qk_t[:, c, :], qk_t[:, c, :], subln[:, 0:1], qk_t[:, DIFF_HEADS + c, :],
                                                         ALU.mult, ALU.mult), b, lam_ready)
            b_ready[c] = split(qk_t[:, c, :], h_hi[:, c, :], h_lo[:, c, :], b, h_reader)
            yield

    units = [{"head": head, "qt": qt, "diff": head < DIFF_HEADS,
              "maps": [2 * head, 2 * head + 1] if head < DIFF_HEADS else [DIFF_HEADS + head]}
             for head in range(DIFF_HEADS + DIL_HEADS) for qt in range(TT)]
    norm_work = diff_norm()
    for n in range(len(units) + 2):
        if n < len(units):
            units[n]["n"] = n
            scores(units[n])
        if 1 <= n <= len(units):
            weights(units[n - 1])
        if n >= 2:
            unit = units[n - 2]
            ready_t = turn(unit)
            if unit["qt"] == TT - 1:
                weigh_values(unit, ready_t)
            if unit["head"] > DIFF_HEADS:
                next(norm_work, None)
    finish(norm_work)

    for n in range(KT):
        bank, token = project(h_hi, h_lo, range(KT), b_ready)
        a = dve.put(lambda e, bank=bank, n=n: e.tensor_tensor(x[:, n, :], bank[:], x[:, n, :], ALU.add), token)
        give(bank, a)
        x_tok[n] = a
    att_done = [token, (act, act.count), (dve, dve.count), (pool, pool.count)]
    att.close()

    swiglu("ffn2_norm_2", att_done, token)
    norm_in_place("final_norm_2", x_tok)
    out_done = counter("out_done")
    for k in range(KT):
        stored = sp.dma(t["out"][:, k, :], x[:, k, :], out_done, x_tok[k])
    sp.wait(stored)
    sp.wait(g_written)
    sp.wait((bias_out, bias_out.count))
    assert used[0] == len(order), (used[0], len(order))
    nc.all_engine_barrier()


def slabs(w):
    k, n = w.shape
    b = w.reshape(k // P, P, n // P, P).transpose(2, 0, 1, 3).reshape(-1, SLAB, P, P)
    return np.ascontiguousarray(b.transpose(0, 2, 1, 3).reshape(-1, P, SLAB * P))


def wide_slabs(w):
    b = w.reshape(w.shape[0] // (2 * P), 2, P, w.shape[1])
    return np.ascontiguousarray(b.transpose(0, 2, 1, 3).reshape(-1, P, SLAB * P))


def columns(v):
    return v.reshape(-1, P).T


def bucket_of(dist):
    n = np.maximum(dist, 0)
    nf = np.maximum(n, 1).astype(np.float32)
    large = 16 + (np.log(nf / 16) / math.log(2048 / 16) * 16).astype(np.int32)
    return np.where(n < 16, n, np.minimum(large, 31))


def windows_of(dist):
    n = sum(((dist >= 0) & (dist % r == 0) & (dist <= w)).astype(np.int32) for w, r in ((128, 1), (512, 4), (2048, 16)))
    return n


def constants():
    i = np.arange(P, dtype=np.float32)
    fix = np.ones((P, CT, PAD_POOL), np.float32)
    for c, w in enumerate(POOL_WINDOWS):
        fix[:, c, :] = w / np.minimum(np.arange(1, PAD_POOL + 1), w)
    dist = S - 1 - np.arange(BIAS_L)
    buckets = np.zeros((DH, 2, BIAS_L), np.float32)
    for kind in range(2):
        buckets[bucket_of(dist), kind, np.arange(BIAS_L)] = 1.0
        buckets[32, kind, :] = (dist < 0) if kind == 0 else (windows_of(dist) == 0)
    z = np.arange(P)[:, None] + (S - P) - np.arange(S)[None, :]
    return {
        "ident": np.eye(P, dtype=np.float32),
        "ones": np.ones((P, P), np.float32),
        "iota128": np.ascontiguousarray(np.broadcast_to(i, (P, P))),
        "iota16": np.ascontiguousarray(np.broadcast_to(i[:TOPK], (P, TOPK))),
        "window_fix": fix,
        "buckets": buckets,
        "mult": windows_of(z).astype(np.float32),
    }


def laid_out(a):
    o = dict(constants())
    o["x"] = np.ascontiguousarray(a["x"][0].T.reshape(KT, P, S).transpose(1, 0, 2))
    vectors = {n: columns(a[n].reshape(-1)) for n in COLS if n != "dw_kernel"}
    vectors["dw_kernel"] = a["dw_kernel"][0].T.reshape(CT, P, CONV_K).transpose(1, 0, 2).reshape(P, -1)
    o["cols"] = np.ascontiguousarray(np.concatenate([vectors[n] for n in COLS], axis=1))
    ada = a["ada_w"][0].reshape(KT, P, 6, D)
    o["ada_w"] = np.ascontiguousarray(ada.transpose(2, 0, 1, 3).reshape(6 * KT, P, D))
    w = a["w_in"][0]
    value_gate = [w[:, CW + half * CW + c * P:CW + half * CW + (c + 1) * P] for c in range(CT) for half in range(2)]
    o["w_in"] = slabs(np.concatenate([w[:, :CW]] + value_gate + [w[:, 3 * CW:]], axis=1))
    o["pool_w"] = np.ascontiguousarray(a["pool_w"][0].transpose(1, 0, 2))
    o["w_merge"] = slabs(np.concatenate([a["pool_up"][0], a["conv_out"][0]], axis=0))
    o["w_out"] = slabs(a["w_out"][0])
    o["w_query"] = slabs(a["w_query"][0])
    o["keys"] = np.ascontiguousarray(np.stack([a["sub_keys_1"][0].T, a["sub_keys_2"][0].T], axis=1))
    u = a["expert_u"][0].reshape(EXPERT_TILES, P, KT, P)
    o["expert_u"] = np.ascontiguousarray(u.transpose(0, 3, 2, 1).reshape(EXPERT_TILES, P, KT * P))
    v = a["expert_v"][0].reshape(N_GROUPS, GROUP, P, KT, P)
    o["expert_v"] = np.ascontiguousarray(v.transpose(0, 3, 2, 1, 4).reshape(N_GROUPS * KT, P, GROUP * P))
    for n in ("ffn1", "ffn2"):
        g = a[f"{n}_w_gate_2"][0].reshape(D, FT, P)
        up = a[f"{n}_w_up_2"][0].reshape(D, FT, P)
        o[f"{n}_gate_up"] = slabs(np.stack([g, up], axis=2).reshape(D, 2 * D_FF))
        o[f"{n}_down"] = slabs(a[f"{n}_w_down_2"][0])
    w = a["w_in_2"][0]
    qa, ka, va, qb, kb, vb = (w[:, i * CW:(i + 1) * CW] for i in range(6))
    o["w_in_2"] = np.concatenate([slabs(np.concatenate([qa, ka, qb, kb], axis=1)), wide_slabs(va), wide_slabs(vb)])
    o["w_out_2"] = slabs(a["w_out_2"][0])
    lam = np.stack([a["lambda_q1_2"][0], a["lambda_q2_2"][0], a["lambda_k1_2"][0], a["lambda_k2_2"][0]])
    o["lam_in"] = np.ascontiguousarray(np.broadcast_to(lam, (P, 4, DH)))
    table = np.zeros((DH, N_MAPS), np.float32)
    table[:32] = a["rel_bias_2"]
    table[32] = NEG
    o["rel_bias"] = table
    return o


def kernel(**inputs):
    import concourse.bacc as bacc
    from concourse.bass_utils import run_bass_kernel_spmd

    arrays = laid_out({n: np.asarray(v) for n, v in inputs.items()})
    nc = bacc.Bacc("TRN2", target_bir_lowering=False, num_devices=1)
    t = {n: nc.dram_tensor(n + "_dram", v.shape, F32, kind="ExternalInput").ap() for n, v in arrays.items()}
    t["out"] = nc.dram_tensor("out_dram", (P, KT, S), F32, kind="ExternalOutput").ap()
    t["g_scratch"] = nc.dram_tensor("g_scratch", (S // CHUNK, P, EXPERT_TILES, CHUNK), F32, kind="Internal").ap()
    t["bias_scratch"] = nc.dram_tensor("bias_scratch", (P, N_MAPS, BIAS_L), F32, kind="Internal").ap()
    build(nc, t)
    r = run_bass_kernel_spmd(nc, [{n + "_dram": v for n, v in arrays.items()}], core_ids=[0])
    out = r.results[0]["out_dram"]
    return np.ascontiguousarray(out.transpose(2, 1, 0).reshape(1, S, D))
```

```python
import math
from collections import deque
from contextlib import ExitStack

import numpy as np

import concourse.bass as bass
from concourse import mybir

F32 = mybir.dt.float32
F32R = mybir.dt.float32r
U32 = mybir.dt.uint32
ALU = mybir.AluOpType
ACT = mybir.ActivationFunctionType
AX_X = mybir.AxisListType.X

P = 128
S = 512
D = 1024
KT = D // P
TT = S // P
POOL_WINDOWS = (2, 4, 8, 16)
PAD_POOL = 16
CONV_K = 31
PAD_CONV = CONV_K - 1
CW = 512
CT = CW // P
HEADS = 8
TOPK = 16
N_KEYS = 128
EXPERT_TILES = N_KEYS
GROUP = 8
N_GROUPS = EXPERT_TILES // GROUP
D_FF = 256 * ((8 * D // 3 + 255) // 256)
FT = D_FF // P
DH = 64
DIFF_HEADS = 4
DIL_HEADS = 8
N_MAPS = 2 * DIFF_HEADS + DIL_HEADS
LAM0 = 0.8 - 0.6 * math.exp(-0.3 * 0)
EPS = 1e-6
NEG = -1.0e30
BIAS_L = 640
SLAB = 8
RAW_SLOTS = 6
SPLIT_SLOTS = 3
GELU_SLOTS = 17
UP_PER_HEAD = (1, 1, 2, 2, 2, 2, 2, 2)
ROUTE_STEPS = 6
UP_FROM = 73
UP_EVERY = 4
UNITS_AHEAD = 4
QK_PAIRS = [(c, 4 + c) for c in range(4)] + [(8 + c, 12 + c) for c in range(4)]
COPY_LAG = 4
HOT_SLOTS = 3
G_TILES = 4
G_SLOTS = 2
CHUNK = 32
TOK4 = 4

COLS = {}
_n = 0
for _name, _w in (("c", 8), ("ada_b", 48), ("norm1_g", 8), ("b_in", 28), ("pool_scale", 4), ("dw_bias", 4),
                  ("conv_ln_g", 4), ("conv_ln_b", 4), ("norm2_g", 8), ("final_g", 8), ("ffn1_norm_2", 8),
                  ("mix_norm_2", 8), ("ffn2_norm_2", 8), ("final_norm_2", 8), ("subln_gain_2", 1),
                  ("dw_kernel", CT * CONV_K)):
    COLS[_name] = (_n, _w)
    _n += _w
N_COLS = _n


class Queue:

    def __init__(self, engine, sem):
        self.engine, self.sem, self.count, self.waited = engine, sem, 0, {}

    def put(self, make, *after, counted=True):
        self.wait(*after)
        instruction = make(self.engine)
        if counted:
            self.count += 1
            instruction.then_inc(self.sem, 1)
        return (self, self.count)

    def wait(self, *after):
        for token in after:
            if token is None:
                continue
            if isinstance(token, list):
                self.wait(*token)
                continue
            source, value = token
            if value > self.waited.get(source, 0):
                self.waited[source] = value
                self.engine.wait_ge(source.sem, value)

    def dma(self, dst, src, counter, *after):
        self.wait(*after)
        counter.count += 16
        self.engine.dma_start(dst, src).then_inc(counter.sem, 16)
        return (counter, counter.count)


class Counter:

    def __init__(self, sem):
        self.sem, self.count = sem, 0


def build(nc, t):
    ctx = ExitStack()
    with ctx:
        program(nc, t, ctx)


def program(nc, t, ctx):
    def sb(name, shape, dt=F32, stack=ctx):
        return stack.enter_context(nc.sbuf_tensor(name, shape, dt))

    def sem(name):
        return ctx.enter_context(nc.semaphore(name))

    def counter(name):
        return Counter(sem(name))

    pe = Queue(nc.tensor, sem("pe_done"))
    act = Queue(nc.scalar, sem("act_done"))
    dve = Queue(nc.vector, sem("dve_done"))
    pool = Queue(nc.gpsimd, sem("pool_done"))
    sp = Queue(nc.sync, sem("sp_done"))

    banks = [ctx.enter_context(nc.psum_tensor(f"bank{i}", [P, S], F32)) for i in range(8)]
    free_banks = deque((b, None) for b in banks)

    def take():
        return free_banks.popleft()

    def give(bank, reader):
        free_banks.append((bank, reader))

    ident = sb("ident", [P, P])
    ones = sb("ones", [P, P])
    iota128 = sb("iota128", [P, P])
    iota16 = sb("iota16", [P, TOPK])
    cols = sb("cols", [P, N_COLS])
    window_fix = sb("window_fix", [P, CT, PAD_POOL])
    mod = sb("mod", [P, 48])
    c_act = sb("c_act", [P, KT])
    gain1 = sb("gain1", [P, KT])
    gain2 = sb("gain2", [P, KT])
    gain_f = sb("gain_f", [P, KT])
    subln = sb("subln", [P, 1])
    eps = sb("eps", [P, 1])

    def col(name, k, w=1):
        base, width = COLS[name]
        assert k + w <= width
        return cols[:, base + k:base + k + w]

    def modc(part, k, w=1):
        return mod[:, part * KT + k:part * KT + k + w]

    x = sb("x", [P, KT, S])
    h_hi = sb("h_hi", [P, KT, S], F32R)
    h_lo = sb("h_lo", [P, KT, S], F32R)
    tmp = sb("tmp", [P, 4, S])
    rstd = sb("rstd", [P, S])
    rstd_2 = sb("rstd_2", [P, S])
    sq_sum = sb("sq_sum", [P, S])
    raw = sb("raw", [P, RAW_SLOTS, SLAB * P])
    w_hi = sb("w_hi", [P, SPLIT_SLOTS, SLAB * P], F32R)
    w_lo = sb("w_lo", [P, SPLIT_SLOTS, SLAB * P], F32R)

    cols_in = counter("cols_in")
    const_in = counter("const_in")
    x_in = counter("x_in")

    cols_ready = act.dma(cols[:], t["cols"], cols_in)
    for dst, name in ((ones, "ones"), (ident, "ident"), (window_fix, "window_fix"), (iota128, "iota128"), (iota16, "iota16")):
        consts_ready = act.dma(dst[:], t[name], const_in)

    eps_ready = pool.put(lambda e: e.memset(eps[:], EPS))

    tmp_reader = [None] * 4
    tmp_turn = [0]

    def scratch():
        i = tmp_turn[0] % 4
        tmp_turn[0] += 1
        return i, tmp[:, i, :], tmp_reader[i]

    background = []

    def run_background():
        for entry in list(background):
            for _ in range(entry[1]):
                if next(entry[0], "end") == "end":
                    background.remove(entry)
                    break

    def finish(generator):
        for entry in list(background):
            if entry[0] is generator:
                background.remove(entry)
        for _ in generator:
            pass

    order = []

    def plan(name, split=True, slabs=None):
        n = t[name].shape[0]
        order.extend((t[name][i], split) for i in (range(n) if slabs is None else slabs))

    plan("ada_w", split=False, slabs=range(16))
    ada_rest = list(range(16, 48))
    for i in range(t["w_in"].shape[0]):
        plan("w_in", slabs=[i])
        if i % 4:
            plan("ada_w", split=False, slabs=[ada_rest.pop(0)])
    for i in range(t["w_merge"].shape[0]):
        plan("w_merge", slabs=[i])
        plan("ada_w", split=False, slabs=[ada_rest.pop(0)])
    plan("ada_w", split=False, slabs=ada_rest)
    plan("w_out")
    u_next = 0
    for h in range(HEADS):
        plan("w_query", slabs=[2 * h, 2 * h + 1])
        plan("expert_u", slabs=range(u_next, u_next + UP_PER_HEAD[h]))
        u_next += UP_PER_HEAD[h]
    plan("expert_u", slabs=range(u_next, GELU_SLOTS))
    u_next = GELU_SLOTS
    for g in range(N_GROUPS):
        plan("expert_v", slabs=range(g * KT, (g + 1) * KT))
        for _ in range(GROUP):
            if u_next < EXPERT_TILES:
                plan("expert_u", slabs=[u_next])
                u_next += 1
    plan("ffn1_gate_up")
    plan("ffn1_down")
    plan("w_in_2", slabs=range(16, 24))
    plan("w_in_2", slabs=[n for pair in QK_PAIRS for n in pair])
    plan("w_out_2")
    plan("ffn2_gate_up")
    plan("ffn2_down")

    raw_in = [counter(f"raw_in{i}") for i in range(RAW_SLOTS)]
    split_reader = [None] * SPLIT_SLOTS
    landed, parts_ready, split_slot = {}, {}, {}
    raw_done = {}
    split_slabs = [i for i in range(len(order)) if order[i][1]]
    n_prepared, n_split, used, closed = [0], [0], [0], [0]
    on_unsplit = [None]
    lo_engine = [dve]

    def load():
        i = len(landed)
        while i < len(order) and (i < RAW_SLOTS or i - RAW_SLOTS in raw_done):
            landed[i] = sp.dma(raw[:, i % RAW_SLOTS, :], order[i][0], raw_in[i % RAW_SLOTS], raw_done.get(i - RAW_SLOTS))
            i += 1

    def prepare():
        i = n_prepared[0]
        n_prepared[0] += 1
        if not order[i][1]:
            raw_done[i] = on_unsplit[0](raw[:, i % RAW_SLOTS, :], landed[i])
            load()
            return
        k = n_split[0] % SPLIT_SLOTS
        n_split[0] += 1
        split_slot[i] = k
        hi, lo, r = w_hi[:, k, :], w_lo[:, k, :], raw[:, i % RAW_SLOTS, :]
        hi_done = act.put(lambda e: e.copy(hi, r), landed[i], split_reader[k])
        raw_done[i] = parts_ready[i] = lo_engine[0].put(lambda e: e.tensor_tensor(lo, r, hi.bitcast(F32), ALU.subtract),
                                               landed[i], hi_done)
        load()

    load()

    def prepare_ahead():
        while n_prepared[0] in landed and n_split[0] < closed[0] + SPLIT_SLOTS:
            prepare()

    def open_slab():
        run_background()
        prepare_ahead()
        used[0] += 1
        return split_slabs[used[0] - 1]

    def close_slab(i, last):
        split_reader[split_slot[i]] = last
        closed[0] += 1

    def three(out, a_hi, a_lo, b_hi, b_lo, start, stop, *after):
        pe.put(lambda e: e.matmul(out, a_hi, b_hi, start=start, stop=False), *after, counted=False)
        pe.put(lambda e: e.matmul(out, a_hi, b_lo, start=False, stop=False), counted=False)
        return pe.put(lambda e: e.matmul(out, a_lo, b_hi, start=False, stop=stop))

    cursor = {"slab": None, "block": SLAB}

    def next_block(width=1):
        if cursor["block"] >= SLAB:
            cursor["slab"], cursor["block"] = open_slab(), 0
        i, b = cursor["slab"], cursor["block"]
        cursor["block"] += width
        k, cut = split_slot[i], slice(b * P, (b + width) * P)
        return i, w_hi[:, k, cut], w_lo[:, k, cut], parts_ready[i], cursor["block"] >= SLAB

    def project_steps(x_hi, x_lo, kts, x_ready):
        bank, reader = take()
        for j, k in enumerate(kts):
            i, hi, lo, token, last = next_block()
            done = three(bank[:], hi, lo, x_hi[:, k, :], x_lo[:, k, :], j == 0, j == len(kts) - 1,
                         token, reader if j == 0 else None, x_ready[k])
            if last:
                close_slab(i, done)
            yield bank, done

    def project(x_hi, x_lo, kts, x_ready):
        for bank, done in project_steps(x_hi, x_lo, kts, x_ready):
            pass
        return bank, done

    def project_both(x_hi, x_lo, x_ready):
        opened = [open_slab(), open_slab()]
        (bank_a, reader_a), (bank_b, reader_b) = take(), take()
        done = {}
        for k in range(KT):
            for i, bank, reader in zip(opened, (bank_a, bank_b), (reader_a, reader_b)):
                hi, lo = (w[:, split_slot[i], k * P:(k + 1) * P] for w in (w_hi, w_lo))
                done[i] = three(bank[:], hi, lo, x_hi[:, k, :], x_lo[:, k, :], k == 0, k == KT - 1,
                                parts_ready[i], reader, x_ready[k])
        for i in opened:
            close_slab(i, done[i])
        prepare_ahead()
        return (bank_a, done[opened[0]]), (bank_b, done[opened[1]])

    def split(src, hi, lo, *after, lo_on=dve):
        a = act.put(lambda e: e.copy(hi, src), *after)
        return lo_on.put(lambda e: e.tensor_tensor(lo, src, hi.bitcast(F32), ALU.subtract), a, *after)

    def feature_sum(tiles, tokens, square=True):
        bank, reader = take()
        for j, (tile, token) in enumerate(zip(tiles, tokens)):
            if square:
                i, sq, r = scratch()
                a = act.put(lambda e, sq=sq, tile=tile: e.activation(sq, tile, ACT.Square), token, r)
                done = pe.put(lambda e, sq=sq, j=j: e.matmul(bank[:], ones[:], sq, start=j == 0, stop=j == len(tiles) - 1),
                              a, reader, consts_ready)
                tmp_reader[i] = done
            else:
                done = pe.put(lambda e, tile=tile, j=j: e.matmul(bank[:], ones[:], tile, start=j == 0, stop=j == len(tiles) - 1),
                              token, reader, consts_ready)
        return bank, done

    rstd_reader = [None]

    def inverse_root(bank, token, width, rstd=rstd):
        b = act.put(lambda e: e.activation(rstd[:], bank[:], ACT.Sqrt, scale=1.0 / width, bias=eps[:]), token, rstd_reader[0], eps_ready)
        give(bank, b)
        return dve.put(lambda e: e.reciprocal(rstd[:], rstd[:]), b)

    squares = {"token": None, "reader": None}

    def add_square(k, last=dve):
        if k == 0:
            squares["token"] = act.put(lambda e: e.activation(sq_sum[:], x[:, 0, :], ACT.Square), x_tok[0], squares["reader"])
            return
        i, sq, r = scratch()
        a = act.put(lambda e: e.activation(sq, x[:, k, :], ACT.Square), x_tok[k], r)
        squares["token"] = tmp_reader[i] = (last if k == KT - 1 else pool).put(
            lambda e: e.tensor_tensor(sq_sum[:], sq_sum[:], sq, ALU.add), a, squares["token"])

    def norm_root(rstd=rstd):
        bank, reader = take()
        done = squares["reader"] = pe.put(lambda e: e.matmul(bank[:], ones[:], sq_sum[:], start=True, stop=True),
                                          squares["token"], reader, consts_ready)
        return inverse_root(bank, done, D, rstd)

    def scaled(k, gain, h_reader):
        hi, lo = h_hi[:, k, :], h_lo[:, k, :]
        a = act.put(lambda e: e.activation(hi, x[:, k, :], ACT.Copy, scale=gain), x_tok[k], h_reader)
        return dve.put(lambda e: e.scalar_tensor_tensor(lo, x[:, k, :], gain, hi.bitcast(F32), ALU.mult, ALU.subtract), a)

    def normed(root, gain, shift, after, h_reader):
        out = []
        scaled = {}

        def scale(k):
            i, s, reader = scratch()
            a = dve.put(lambda e: e.scalar_tensor_tensor(s, x[:, k, :], gain(k), rstd[:], ALU.mult, ALU.mult),
                        root, reader, after)
            rstd_reader[0] = a
            hi = h_hi[:, k, :]
            if shift is None:
                b = act.put(lambda e: e.copy(hi, s), a, h_reader)
            else:
                b = act.put(lambda e: e.activation(hi, s, ACT.Identity, bias=shift(k)), a, h_reader)
            scaled[k] = (i, s, b)

        scale(0)
        for k in range(KT):
            if k + 1 < KT:
                scale(k + 1)
            i, s, b = scaled.pop(k)
            hi, lo = h_hi[:, k, :], h_lo[:, k, :]
            if shift is None:
                done = (pool if k % 3 == 2 else dve).put(lambda e: e.tensor_tensor(lo, s, hi.bitcast(F32), ALU.subtract), b)
            else:
                done = dve.put(lambda e: e.scalar_tensor_tensor(lo, s, shift(k), hi.bitcast(F32), ALU.add, ALU.subtract), b)
            tmp_reader[i] = done
            out.append(done)
        return out

    c_ready = act.put(lambda e: e.activation(c_act[:], col("c", 0, 8), ACT.Sigmoid), cols_ready)
    c_ready = dve.put(lambda e: e.tensor_tensor(c_act[:], c_act[:], col("c", 0, 8), ALU.mult), c_ready)
    x_ready = act.dma(x[:], t["x"], x_in)

    mix = ExitStack()
    ada_acc = sb("ada_acc", [P, 2, D], stack=mix)
    x_tok = [x_ready] * KT
    for k in range(KT):
        add_square(k, last=pool)

    ada = {"n": 0, "token": None, "reader": [None, None], "ready": {}}

    def ada_step(w, landed_w):
        part, k = divmod(ada["n"], KT)
        c = c_act[:, k:k + 1]
        acc = ada_acc[:, part % 2, :]
        if k == 0:
            ada["token"] = dve.put(lambda e: e.tensor_scalar(acc, w, c, None, ALU.mult), landed_w, c_ready, ada["reader"][part % 2])
        else:
            ada["token"] = dve.put(lambda e: e.scalar_tensor_tensor(acc, w, c, acc, ALU.mult, ALU.add), landed_w, ada["token"])
        if k == KT - 1:
            ada["summed"] = (part, ada["token"])
        ada["n"] += 1
        if k == 3 and part > 2:
            ada_sums()
        return ada["token"]

    def ada_sums():
        part, token = ada["summed"]
        acc = ada_acc[:, part % 2, :]
        bank, reader = take()
        for n in range(KT):
            done = pe.put(lambda e: e.matmul(bank[:, n:n + 1], acc[:, n * P:(n + 1) * P], ones[:, 0:1], start=True, stop=True),
                          token, reader, consts_ready)
        ada["reader"][part % 2] = done
        ada["ready"][part] = dve.put(lambda e: e.tensor_tensor(
            mod[:, part * KT:(part + 1) * KT], bank[:, 0:KT], col("ada_b", part * KT, KT), ALU.add), done, consts_ready)
        give(bank, ada["ready"][part])

    on_unsplit[0] = ada_step
    for _ in range(KT):
        prepare()
    ada_sums()
    for _ in range(KT - 2):
        prepare()
    root = norm_root()
    for _ in range(2):
        prepare()
    ada_sums()
    prepare_ahead()
    gain1_ready = dve.put(lambda e: e.scalar_tensor_tensor(gain1[:], modc(1, 0, KT), 1.0, col("norm1_g", 0, KT), ALU.add, ALU.mult),
                          ada["ready"][1])
    h_ready = normed(root, lambda k: gain1[:, k:k + 1], lambda k: modc(0, k), [x_ready, gain1_ready], None)

    gates = sb("gates", [P, 2 * KT, S], stack=mix)
    conv = sb("conv", [P, CT, S], stack=mix)
    mixed = sb("mixed", [P, CT, S], stack=mix)
    pool_w = sb("pool_w", [P, CT, P], stack=mix)
    front = ExitStack()
    p_pad = sb("p_pad", [P, CT, PAD_POOL + S], stack=front)
    a_val = sb("a_val", [P, S], stack=front)
    glu = sb("glu", [P, CT, PAD_CONV + S], stack=front)
    pooled = sb("pooled", [P, 2, PAD_POOL + S], stack=front)
    prod = sb("prod", [P, 2, S], stack=front)

    pads = pool.put(lambda e: e.memset(p_pad[:, :, 0:PAD_POOL], 0.0))
    pads = pool.put(lambda e: e.memset(glu[:, :, 0:PAD_CONV], 0.0))

    p_ready = []
    for c in range(CT):
        if c % 2 == 0:
            pair = project_both(h_hi, h_lo, h_ready)
        bank, token = pair[c % 2]
        a = act.put(lambda e, bank=bank, c=c: e.activation(p_pad[:, c, PAD_POOL:], bank[:], ACT.Identity, bias=col("b_in", c)), token)
        give(bank, a)
        p_ready.append(a)

    mixed_ready = []
    pool_prev = None
    for c, w in enumerate(POOL_WINDOWS):
        src, token, shift, lv = p_pad[:, c, :], [p_ready[c], pads, pool_prev], 1, 0
        lo_col = 0
        while shift < w:
            lo_col += shift
            dst = pooled[:, lv % 2, :]
            token = pool.put(lambda e, dst=dst, src=src, shift=shift, lo_col=lo_col: e.tensor_tensor(
                dst[:, lo_col:], src[:, lo_col:], src[:, lo_col - shift:PAD_POOL + S - shift], ALU.add), token)
            src, shift, lv = dst, shift * 2, lv + 1
        body = mixed[:, c, :]
        a = pool.put(lambda e, body=body, src=src, w=w: e.tensor_scalar(body, src[:, PAD_POOL:], 1.0 / w, None, ALU.mult), token)
        a = pool.put(lambda e, body=body, c=c: e.tensor_tensor(body[:, 0:PAD_POOL], body[:, 0:PAD_POOL], window_fix[:, c, :], ALU.mult),
                     a, consts_ready)
        pool_prev = pool.put(lambda e, body=body, c=c: e.tensor_tensor(body, body, p_pad[:, c, PAD_POOL:], ALU.subtract), a)
        mixed_ready.append(pool_prev)

    conv_token = [None] * CT
    prod_reader = [None, None]

    def convolve():
        for pair in ((0, 1), (2, 3)):
            if pair[0]:
                lo_engine[0] = pool
            for j in range(CONV_K):
                for c in pair:
                    tap = col("dw_kernel", c * CONV_K + j)
                    src = glu[:, c, j:j + S]
                    acc = conv[:, c, :]
                    if c != 1 and j == 0:
                        conv_token[c] = dve.put(lambda e: e.tensor_scalar(acc, src, tap, col("dw_bias", c), ALU.mult, ALU.add),
                                                glu_ready[c], pads)
                    elif c != 1:
                        conv_token[c] = dve.put(lambda e: e.scalar_tensor_tensor(acc, src, tap, acc, ALU.mult, ALU.add), conv_token[c])
                    elif j == 0:
                        conv_token[c] = act.put(lambda e: e.activation(acc, src, ACT.Identity, scale=tap, bias=col("dw_bias", c)),
                                                glu_ready[c], pads)
                    else:
                        one = prod[:, j % 2, :]
                        a = act.put(lambda e: e.activation(one, src, ACT.Copy, scale=tap), glu_ready[c], pads, prod_reader[j % 2])
                        conv_token[c] = prod_reader[j % 2] = pool.put(lambda e: e.tensor_tensor(acc, acc, one, ALU.add),
                                                                      a, conv_token[c])
                yield
        lo_engine[0] = dve

    front_done = []

    def branches():
        for _ in convolve():
            yield
        front_done.extend(conv_token + [pool_prev])
        bank, token = feature_sum([conv[:, c, :] for c in range(CT)], conv_token, square=False)
        yield
        yield
        for c in range(CT):
            a = dve.put(lambda e: e.scalar_tensor_tensor(conv[:, c, :], bank[:], -1.0 / CW, conv[:, c, :], ALU.mult, ALU.add), token)
            conv_token[c] = a
        give(bank, a)
        yield
        bank, token = feature_sum([conv[:, c, :] for c in range(CT)], conv_token)
        yield
        for c in range(CT):
            bank_g, reader = take()
            a = pe.put(lambda e: e.matmul(bank_g[:], pool_w[:, c, :], mixed[:, c, :], start=True, stop=True),
                       mixed_ready[c], pool_w_ready, reader)
            i, s, r = scratch()
            a = dve.put(lambda e: e.tensor_scalar(s, bank_g[:], col("pool_scale", c), None, ALU.mult), a, r)
            give(bank_g, a)
            b_ready[c] = tmp_reader[i] = split(s, b_hi[:, c, :], b_lo[:, c, :], a, front_done)
            yield
        root = inverse_root(bank, token, CW)
        yield
        sigmoids = []
        for c in range(CT):
            a = dve.put(lambda e: e.scalar_tensor_tensor(conv[:, c, :], conv[:, c, :], col("conv_ln_g", c), rstd[:], ALU.mult, ALU.mult), root)
            rstd_reader[0] = a
            i, s, rd = scratch()
            b = act.put(lambda e: e.activation(s, conv[:, c, :], ACT.Sigmoid, bias=col("conv_ln_b", c)), a, rd)
            sigmoids.append((i, s, b))
        for c, (i, s, b) in enumerate(sigmoids):
            b = dve.put(lambda e: e.scalar_tensor_tensor(s, conv[:, c, :], col("conv_ln_b", c), s, ALU.add, ALU.mult), b)
            b_ready[CT + c] = tmp_reader[i] = split(s, b_hi[:, CT + c, :], b_lo[:, CT + c, :], b, front_done)
            yield

    pool_w_in = counter("pool_w_in")
    pool_w_ready = act.dma(pool_w[:], t["pool_w"], pool_w_in)
    branch_work = branches()

    glu_ready = []
    a_val_reader = None
    for c in range(CT):
        bank, token = project(h_hi, h_lo, range(KT), h_ready)
        a = act.put(lambda e, bank=bank, c=c: e.activation(a_val[:], bank[:], ACT.Identity, bias=col("b_in", CT + c)),
                    token, a_val_reader)
        give(bank, a)
        bank, token = project(h_hi, h_lo, range(KT), h_ready)
        i, s, r = scratch()
        b = act.put(lambda e, bank=bank, s=s, c=c: e.activation(s, bank[:], ACT.Sigmoid, bias=col("b_in", 2 * CT + c)), token, r)
        give(bank, b)
        a_val_reader = dve.put(lambda e, s=s, c=c: e.tensor_tensor(glu[:, c, PAD_CONV:], a_val[:], s, ALU.mult), b, a)
        tmp_reader[i] = a_val_reader
        glu_ready.append(a_val_reader)
        if c == 1:
            background.append([branch_work, 3])

    front.close()
    b_hi = sb("b_hi", [P, KT, S], F32R, stack=mix)
    b_lo = sb("b_lo", [P, KT, S], F32R, stack=mix)
    b_ready = [None] * KT
    gate_ready = []
    for n in range(2 * KT):
        bank, token = project(h_hi, h_lo, range(KT), h_ready)
        a = act.put(lambda e, bank=bank, n=n: e.activation(gates[:, n, :], bank[:], ACT.Sigmoid, bias=col("b_in", 3 * CT + n)), token)
        give(bank, a)
        gate_ready.append(a)
    finish(branch_work)
    h_reader = token

    merged_ready = []
    for n in range(KT):
        bank_p, token_p = project(b_hi, b_lo, range(CT), b_ready)
        bank_c, token_c = project(b_hi, b_lo, range(CT, KT), b_ready)
        i, s, r = scratch()
        a = dve.put(lambda e, s=s, n=n, bank=bank_p: e.tensor_tensor(s, bank[:], gates[:, n, :], ALU.mult), token_p, r, gate_ready[n])
        give(bank_p, a)
        i2, s2, r2 = scratch()
        b = dve.put(lambda e, s2=s2, n=n, bank=bank_c: e.tensor_tensor(s2, bank[:], gates[:, KT + n, :], ALU.mult), token_c, r2, gate_ready[KT + n])
        give(bank_c, b)
        c_ = pool.put(lambda e, s=s, s2=s2: e.tensor_tensor(s, s, s2, ALU.add), a, b)
        tmp_reader[i2] = c_
        done = split(s, h_hi[:, n, :], h_lo[:, n, :], c_, h_reader)
        tmp_reader[i] = done
        merged_ready.append(done)

    ada_sums()
    for n in range(KT):
        bank, token = project(h_hi, h_lo, range(KT), merged_ready)
        a = dve.put(lambda e, bank=bank, n=n: e.scalar_tensor_tensor(x[:, n, :], bank[:], modc(2, n), x[:, n, :], ALU.mult, ALU.add), token)
        give(bank, a)
        x_tok[n] = a
        add_square(n)
    mix_done = [token, a, pool_prev, act.put(lambda e: e.copy(gain2[:], gain1[:]))]
    mix.close()

    gain2_ready = dve.put(lambda e: e.scalar_tensor_tensor(gain2[:], modc(4, 0, KT), 1.0, col("norm2_g", 0, KT), ALU.add, ALU.mult),
                          mix_done)
    h_ready = normed(norm_root(), lambda k: gain2[:, k:k + 1], lambda k: modc(3, k), gain2_ready, token)

    peer = ExitStack()
    gelu = sb("gelu", [P, GELU_SLOTS, S], stack=peer)
    staging = ExitStack()
    sel_t = sb("sel_t", [P, 3, S], stack=staging)
    neg_t = sb("neg_t", [P, 2, S], stack=staging)
    hot2 = sb("hot2", [P, HOT_SLOTS, TOK4, P], stack=staging)
    hot1 = sb("hot1", [P, HOT_SLOTS, TOK4, P], stack=staging)
    choosing = ExitStack()
    sel_s = sb("sel_s", [P, TT, HEADS, TOPK], stack=choosing)
    sel_i = sb("sel_i", [P, 2, TT, HEADS, TOPK], stack=choosing)
    soft = sb("soft", [P, TT * HEADS], stack=choosing)
    keys = sb("keys", [P, 2, P], stack=choosing)
    q_t = sb("q_t", [P, 2, 2, S], stack=choosing)
    top = sb("top", [P, TT, 2, TOPK], stack=choosing)
    top_u = sb("top_u", [P, TT, 2, TOPK], U32, stack=choosing)
    top_f = sb("top_f", [P, TT, 2, TOPK], stack=choosing)
    rest = sb("rest", [P, TT, 2 * P], stack=choosing)
    cand = sb("cand", [P, TT, TOPK, TOPK], stack=choosing)
    pos = sb("pos", [P, TT, TOPK], U32, stack=choosing)
    pos_u = sb("pos_u", [P, 2, TT, TOPK], U32, stack=choosing)
    pos_f = sb("pos_f", [P, 2, TT, TOPK], stack=choosing)
    keys_in = counter("keys_in")
    keys_ready = act.dma(keys[:], t["keys"], keys_in, *mix_done)

    routed = []

    q_reader = [None, None]
    q_ready = [[] for h in range(HEADS)]

    def best_sixteen(scores, values, places, n, after):
        tiles = range(TT)
        first = [dve.put(lambda e: e.max(values[i][:, 0:8], scores[i]), *after) for i in tiles]
        yield
        left = [dve.put(lambda e: e.match_replace(rest[:, i, 0:n], values[i][:, 0:8], scores[i], NEG), first[i]) for i in tiles]
        yield
        for i in tiles:
            dve.put(lambda e: e.max_index(places[i][:, 0:8], values[i][:, 0:8], scores[i]), first[i])
        yield
        second = [dve.put(lambda e: e.max(values[i][:, 8:16], rest[:, i, 0:n]), left[i]) for i in tiles]
        yield
        for i in tiles:
            dve.put(lambda e: e.max_index(places[i][:, 8:16], values[i][:, 8:16], rest[:, i, 0:n]), second[i])
        yield

    def route(h):
        bank_of = []
        for half in range(2):
            bank, reader = take()
            for tt in range(TT):
                a = pe.put(lambda e, bank=bank, half=half, tt=tt: e.matmul(
                    bank[:, tt * P:(tt + 1) * P], q_t[:, h % 2, half, tt * P:(tt + 1) * P], keys[:, half, :], start=True, stop=True),
                    q_ready[h][half], reader, keys_ready, mix_done)
            bank_of.append((bank, a))
        q_reader[h % 2] = a
        last = None
        for half in range(2):
            bank, token = bank_of[half]
            s = [bank[:, tt * P:(tt + 1) * P] for tt in range(TT)]
            for step in best_sixteen(s, [top[:, tt, half, :] for tt in range(TT)], [top_u[:, tt, half, :] for tt in range(TT)],
                                     P, [token, routed[-1:] or mix_done]):
                yield
            last = (dve, dve.count)
            give(bank, last)
        top_ready = dve.put(lambda e: e.tensor_copy(top_f[:], top_u[:]), last)
        one = top[:, :, 0, :].unsqueeze(3).to_broadcast([P, TT, TOPK, TOPK])
        two = top[:, :, 1, :].unsqueeze(2).to_broadcast([P, TT, TOPK, TOPK])
        cand_ready = dve.put(lambda e: e.tensor_tensor(cand[:], one, two, ALU.add), last)
        yield
        for step in best_sixteen([cand[:, tt, :, :].rearrange("p a b -> p (a b)") for tt in range(TT)],
                                 [sel_s[:, tt, h, :] for tt in range(TT)], [pos[:, tt, :] for tt in range(TT)], 2 * P, [cand_ready]):
            yield
        last = (dve, dve.count)
        a = dve.put(lambda e: e.tensor_single_scalar(pos_u[:, 0], pos[:], 4, ALU.logical_shift_right), last)
        b = dve.put(lambda e: e.tensor_single_scalar(pos_u[:, 1], pos[:], TOPK - 1, ALU.bitwise_and), last)
        pos_ready = dve.put(lambda e: e.tensor_copy(pos_f[:], pos_u[:]), b)
        yield
        iota_b = iota16[:].unsqueeze(1).unsqueeze(1).to_broadcast([P, TT, TOPK, TOPK])
        hits = [cand[:], rest[:].rearrange("p t (a b) -> p t a b", a=TOPK)]
        tf = [top_f[:, :, half, :].unsqueeze(2).to_broadcast([P, TT, TOPK, TOPK]) for half in range(2)]
        hit = []
        for half in range(2):
            pf = pos_f[:, half].unsqueeze(3).to_broadcast([P, TT, TOPK, TOPK])
            hit.append(dve.put(lambda e: e.tensor_tensor(hits[half], pf, iota_b, ALU.is_equal), pos_ready, consts_ready, top_ready, last))
        first = pool.put(lambda e: e.tensor_tensor(hits[0], hits[0], tf[0], ALU.mult), hit[0])
        yield
        second = dve.put(lambda e: e.tensor_tensor(hits[1], hits[1], tf[1], ALU.mult), hit[1])
        dve.put(lambda e: e.tensor_reduce(sel_i[:, 1, :, h, :], hits[1], AX_X, ALU.add), second)
        last = dve.put(lambda e: e.tensor_reduce(sel_i[:, 0, :, h, :], hits[0], AX_X, ALU.add), first)
        yield
        routed.append(last)

    gelu_reader = [mix_done] * GELU_SLOTS
    gelu_ready = {}

    def expert_up_steps(b):
        for bank, token in project_steps(h_hi, h_lo, range(KT), h_ready):
            yield
        s = b % GELU_SLOTS
        gelu_ready[b] = act.put(lambda e, bank=bank, s=s: e.activation(gelu[:, s, :], bank[:], ACT.Gelu_apprx_tanh), token, gelu_reader[s])
        give(bank, gelu_ready[b])

    def expert_up(b):
        for _ in expert_up_steps(b):
            pass

    lo_engine[0] = pool
    route_work = []
    for h in range(HEADS):
        pair = project_both(h_hi, h_lo, h_ready) if h == 0 else None
        for half in range(2):
            bank, token = pair[half] if pair else project(h_hi, h_lo, range(KT), h_ready)
            a = act.put(lambda e, bank=bank, half=half: e.copy(q_t[:, h % 2, half, :], bank[:]), token, q_reader[h % 2], mix_done)
            give(bank, a)
            q_ready[h].append(a)
        if route_work:
            finish(route_work[-1])
        work = route(h)
        route_work.append(work)
        background.append([work, ROUTE_STEPS])
        for _ in range(UP_PER_HEAD[h]):
            expert_up(len(gelu_ready))

    g_dram = t["g_scratch"]
    chunk_out = [counter("chunk_out0"), counter("chunk_out1")]
    chunk_out_done = [None, None]

    def routing_matrix():
        v = sel_s[:].rearrange("p t h k -> p (t h) k")
        best = sel_s[:, :, :, 0:1].rearrange("p t h k -> p (t h) k").to_broadcast([P, TT * HEADS, TOPK])
        e_ = cand[:].rearrange("p t a b -> p (t a b)")[:, 0:TT * HEADS * TOPK].rearrange("p (g k) -> p g k", k=TOPK)
        a = dve.put(lambda e: e.tensor_tensor(e_, v, best, ALU.subtract), routed[-1])
        a = act.put(lambda e: e.activation(e_, e_, ACT.Exp), a)
        b = dve.put(lambda e: e.tensor_reduce(soft[:], e_, AX_X, ALU.add), a)
        b = dve.put(lambda e: e.reciprocal(soft[:], soft[:]), b)
        gate = dve.put(lambda e: e.tensor_tensor(v, e_, soft[:].unsqueeze(2).to_broadcast([P, TT * HEADS, TOPK]), ALU.mult), b)
        yield
        sel_ready = []
        for n, src in enumerate((sel_s[:], sel_i[:, 0], sel_i[:, 1])):
            bank, reader = take()
            for tt in range(TT):
                a = pe.put(lambda e, bank=bank, tt=tt, src=src: e.transpose(
                    bank[:, tt * P:(tt + 1) * P], src[:, tt].rearrange("p h k -> p (h k)"), ident[:]), gate, reader, consts_ready)
            a = act.put(lambda e, bank=bank, n=n: e.copy(sel_t[:, n, :], bank[:]), a)
            give(bank, a)
            sel_ready.append(a)
            if n < 2:
                sel_ready.append(act.put(lambda e: e.mul(neg_t[:, n, :], sel_t[:, n, :], -1.0), a))
        stage_free = [gate, q_reader, sel_ready]
        choosing.close()
        stage_all = sb("stage", [P, 2, P, CHUNK], stack=staging)
        yield
        hot_reader = [None] * HOT_SLOTS
        hot_ready, distance, summed = {}, {}, {}

        def one_hots(g):
            r, t0 = g % HOT_SLOTS, g * TOK4
            key2 = sel_t[:, 2, t0:t0 + TOK4].unsqueeze(2).to_broadcast([P, TOK4, P])
            hot_ready[g] = [dve.put(lambda e: e.tensor_tensor(
                hot2[:, r], iota128[:].unsqueeze(1).to_broadcast([P, TOK4, P]), key2, ALU.is_equal), sel_ready, hot_reader[r])]
            for j in range(TOK4):
                one, key1, gate1 = hot1[:, r, j, :], sel_t[:, 1, t0 + j:t0 + j + 1], sel_t[:, 0, t0 + j:t0 + j + 1]
                if j == 3:
                    b = act.put(lambda e: e.activation(one, iota128[:], ACT.Abs, bias=neg_t[:, 1, t0 + j:t0 + j + 1]),
                                sel_ready, hot_reader[r])
                    distance[g] = (one, gate1, neg_t[:, 0, t0 + j:t0 + j + 1], b)
                else:
                    b = (pool if j == 0 else dve).put(lambda e: e.tensor_scalar(one, iota128[:], key1, gate1, ALU.is_equal, ALU.mult),
                                                      sel_ready, hot_reader[r])
                    hot_ready[g].append(b)

        def last_hot(g):
            one, gate1, minus_gate, after = distance.pop(g)
            hot_ready[g].append(act.put(lambda e: e.activation(one, one, ACT.Relu, bias=gate1, scale=minus_gate), after))

        def routing_products(g):
            r = g % HOT_SLOTS
            bank, reader = take()
            for j in range(TOK4):
                c = pe.put(lambda e: e.matmul(bank[:, j * P:(j + 1) * P], hot2[:, r, j, :], hot1[:, r, j, :], start=True, stop=True),
                           hot_ready[g], reader)
            hot_reader[r] = c
            summed[g] = (bank, c)

        def to_chunk(g):
            t0 = g * TOK4
            o, half = t0 % CHUNK, t0 // CHUNK % 2
            bank, c = summed.pop(g)
            done = act.put(lambda e: e.copy(
                stage_all[:, half, :, o:o + TOK4].rearrange("p b t -> p t b"), bank[:].rearrange("p (t b) -> p t b", t=TOK4)),
                c, chunk_out_done[half], stage_free)
            give(bank, done)
            if o + TOK4 == CHUNK:
                chunk_out_done[half] = act.dma(g_dram[t0 // CHUNK], stage_all[:, half], chunk_out[half], done)

        groups = S // TOK4
        for step in range(groups + COPY_LAG):
            if step < groups:
                one_hots(step)
            if step >= COPY_LAG:
                to_chunk(step - COPY_LAG)
            if step < groups:
                last_hot(step)
            if 0 <= step - 1 < groups:
                routing_products(step - 1)
            yield
        g_written.extend(chunk_out_done)

    g_written = []
    matrix_work = routing_matrix()
    finish(route_work[-1])
    up_work = (None for b in range(len(gelu_ready), GELU_SLOTS) for _ in expert_up_steps(b))
    for step, _ in enumerate(matrix_work):
        if step >= UP_FROM and step % UP_EVERY == 0:
            next(up_work, None)
    for _ in up_work:
        pass
    lo_engine[0] = dve

    staging.close()
    g_tile = sb("g_tile", [P, G_SLOTS, S // CHUNK, G_TILES, CHUNK], stack=peer)
    act_hi = sb("act_hi", [P, GROUP, S], F32R, stack=peer)
    act_lo = sb("act_lo", [P, GROUP, S], F32R, stack=peer)
    table = sb("table", [DH, N_MAPS], stack=peer)
    buckets = sb("buckets", [DH, 2, BIAS_L], stack=peer)
    by_dist = sb("by_dist", [DIL_HEADS, 2, BIAS_L], stack=peer)
    table_in = counter("table_in")
    bias_out = counter("bias_out")
    b_dram = t["bias_scratch"]

    def relative_bias():
        sp.dma(table[:], t["rel_bias"], table_in, g_written)
        ready = sp.dma(buckets[:], t["buckets"], table_in, g_written)
        for kind in range(2):
            for width, off in ((S, 0), (BIAS_L - S, S)):
                bank, reader = take()
                a = pe.put(lambda e: e.matmul(
                    bank[0:DIL_HEADS, 0:width], table[:, kind * 8:kind * 8 + 8], buckets[:, kind, off:off + width],
                    start=True, stop=True), ready, reader)
                a = act.put(lambda e: e.mul(by_dist[:, kind, off:off + width], bank[0:DIL_HEADS, 0:width], DH ** 0.5), a, g_written)
                give(bank, a)
            out = act.dma(b_dram[:, kind * 8:kind * 8 + 8, :].rearrange("q m x -> m q x"),
                          by_dist[:, kind, :].unsqueeze(1).to_broadcast([DIL_HEADS, P, BIAS_L]), bias_out, a)
        return out

    g_in = [counter(f"g_in{i}") for i in range(G_SLOTS)]
    g_reader = [g_written] * G_SLOTS
    g_landed = {}
    w_ready = {}
    v_last = [None]

    def load_g(n):
        if n * G_TILES < EXPERT_TILES:
            s = n % G_SLOTS
            g_landed[n] = sp.dma(g_tile[:, s].rearrange("p c b t -> p c (b t)"),
                                 g_dram[:, :, n * G_TILES:(n + 1) * G_TILES, :].rearrange("c p b t -> p c (b t)"),
                                 g_in[s], g_written, g_reader[s])

    weighed = {}

    def weigh(b):
        s, n = b % GELU_SLOTS, b // G_TILES
        src = gelu[:, s, :]
        g_b = g_tile[:, n % G_SLOTS, :, b % G_TILES, :]
        a = dve.put(lambda e: e.tensor_tensor(src.rearrange("p (c t) -> p c t", t=CHUNK), src.rearrange("p (c t) -> p c t", t=CHUNK),
                                              g_b, ALU.mult), gelu_ready[b], g_landed[n])
        if b % G_TILES == G_TILES - 1:
            g_reader[n % G_SLOTS] = a
            load_g(n + G_SLOTS)
        weighed[b] = a

    def split_weighed(b):
        s, k = b % GELU_SLOTS, b % GROUP
        w_ready[b] = gelu_reader[s] = split(gelu[:, s, :], act_hi[:, k, :], act_lo[:, k, :], weighed.pop(b), v_last[0], g_written)

    for n in range(G_SLOTS):
        load_g(n)
    weigh(0)
    for b in range(GROUP):
        if b + 1 < GROUP:
            weigh(b + 1)
        split_weighed(b)
    u_next = GELU_SLOTS
    gain_ready = dve.put(lambda e: e.tensor_tensor(gain_f[:], col("final_g", 0, KT), col("ffn1_norm_2", 0, KT), ALU.mult))
    act.wait(gain_ready)
    for g in range(N_GROUPS):
        ready_w = [w_ready[g * GROUP + j] for j in range(GROUP)]
        for dt in range(KT):
            bank, token = project(act_hi, act_lo, range(GROUP), ready_w)
            x_tok[dt] = dve.put(lambda e, bank=bank, dt=dt: e.scalar_tensor_tensor(
                x[:, dt, :], bank[:], modc(5, dt), x[:, dt, :], ALU.mult, ALU.add), token, x_tok[dt])
            give(bank, x_tok[dt])
            if g == N_GROUPS - 1:
                add_square(dt)
                h_ready[dt] = scaled(dt, gain_f[:, dt:dt + 1], up_done)
        v_last[0] = token
        if g == 1:
            b_out = relative_bias()
        for j in range(GROUP):
            if u_next < EXPERT_TILES:
                expert_up(u_next)
                up_done = (pe, pe.count)
                u_next += 1
            if g + 1 < N_GROUPS:
                weigh((g + 1) * GROUP + j)
                if j:
                    split_weighed((g + 1) * GROUP + j - 1)
                if j == GROUP - 1:
                    split_weighed((g + 1) * GROUP + j)
    peer_done = [token, b_out, (act, act.count), (dve, dve.count), (pool, pool.count)]
    peer.close()

    def norm_in_place(name, root, tiles=range(KT)):
        for k in tiles:
            x_tok[k] = rstd_reader[0] = dve.put(lambda e: e.scalar_tensor_tensor(
                x[:, k, :], x[:, k, :], col(name, k), rstd[:], ALU.mult, ALU.mult), root, x_tok[k])

    def swiglu(name, place_free, hr, scale, roots):
        ffn = ExitStack()
        f_hi = sb(name + "_f_hi", [P, FT, S], F32R, stack=ffn)
        f_lo = sb(name + "_f_lo", [P, FT, S], F32R, stack=ffn)
        f_ready, pairs, scale_ready = [], deque(), None
        for n in range(FT):
            if n == 0:
                pairs.append(project_both(h_hi, h_lo, hr))
            else:
                pairs.append((project(h_hi, h_lo, range(KT), hr), project(h_hi, h_lo, range(KT), hr)))
            prepare_ahead()
            if scale_ready is None:
                scale_ready = next(roots)
            while pairs and scale_ready:
                (bank_g, token_g), (bank_u, token_u) = pairs.popleft()
                n = len(f_ready)
                (i, s, r), (i2, s2, r2) = scratch(), scratch()
                a = dve.put(lambda e: e.tensor_tensor(s, bank_g[:], scale[:], ALU.mult), token_g, r, scale_ready)
                give(bank_g, a)
                b = act.put(lambda e: e.activation(s, s, ACT.Silu), a)
                a = rstd_reader[0] = dve.put(lambda e: e.tensor_tensor(s2, bank_u[:], scale[:], ALU.mult), token_u, r2)
                give(bank_u, a)
                tmp_reader[i2] = b = dve.put(lambda e: e.tensor_tensor(s, s, s2, ALU.mult), a, b)
                tmp_reader[i] = split(s, f_hi[:, n, :], f_lo[:, n, :], b, place_free)
                f_ready.append(tmp_reader[i])
        for n in range(KT):
            bank, token = project(f_hi, f_lo, range(FT), f_ready)
            a = dve.put(lambda e: e.scalar_tensor_tensor(x[:, n, :], bank[:], 0.5, x[:, n, :], ALU.mult, ALU.add), token, x_tok[n])
            give(bank, a)
            x_tok[n] = a
            add_square(n)
        ffn.close()
        return token_u, token

    def two_roots():
        first = norm_root()
        yield None
        for k in range(KT):
            norm_in_place("final_g", first, [k])
            add_square(k)
        yield None
        second = norm_root(rstd_2)
        yield dve.put(lambda e: e.tensor_tensor(rstd_2[:], rstd_2[:], rstd[:], ALU.mult), second)

    def one_root():
        yield norm_root()

    h_reader, f_reader = swiglu("ffn1", peer_done, h_ready, rstd_2, two_roots())

    att = ExitStack()
    qk_t = sb("qk_t", [P, 16, S], stack=att)
    v_nat = sb("v_nat", [P, TT, D], stack=att)
    bias = sb("bias", [P, 4, S], stack=att)
    mult = sb("mult", [P, S], stack=att)
    lam_in = sb("lam_in", [P, 4, DH], stack=att)
    lam = sb("lam", [P, 8], stack=att)
    stat = sb("stat", [P, 2 * TT * N_MAPS], stack=att)
    att_in = counter("att_in")
    bias_in = [counter(f"bias_in{i}") for i in range(4)]

    old = [f_reader, (act, act.count)]
    for dst, name in ((mult, "mult"), (lam_in, "lam_in")):
        att_ready = sp.dma(dst[:], t[name], att_in, *old)
    root = norm_root()
    bias_reader = [old] * 4
    bias_ready = {}

    def load_bias(m):
        if m < N_MAPS:
            skew = bass.AP(b_dram.tensor, m * BIAS_L + P - 1, [[N_MAPS * BIAS_L - 1, P], [1, S]])
            bias_ready[m] = pool.dma(bias[:, m % 4, :], skew, bias_in[m % 4], b_out, bias_reader[m % 4])

    for m in range(4):
        load_bias(m)

    h_ready = normed(root, lambda k: col("mix_norm_2", k), None, None, h_reader)
    a = dve.put(lambda e: e.tensor_tensor(lam_in[:, 0:2, :], lam_in[:, 0:2, :], lam_in[:, 2:4, :], ALU.mult), att_ready)
    a = dve.put(lambda e: e.tensor_reduce(lam[:, 0:2], lam_in[:, 0:2, :], AX_X, ALU.add), a)
    a = act.put(lambda e: e.activation(lam[:, 2:4], lam[:, 0:2], ACT.Exp), a)
    a = dve.put(lambda e: e.tensor_tensor(lam[:, 4:5], lam[:, 2:3], lam[:, 3:4], ALU.subtract), a)
    a = dve.put(lambda e: e.tensor_scalar(lam[:, 5:6], lam[:, 4:5], LAM0, None, ALU.add), a)
    lam_ready = dve.put(lambda e: e.tensor_scalar(subln[:], col("subln_gain_2", 0), 1.0 - LAM0, None, ALU.mult), a)

    v_ready = None
    for half in range(2):
        four = [take() for _ in range(TT)]
        for k in range(KT):
            i, w_h, w_l, token, last = next_block(4)
            for tt in range(TT):
                cut = slice(tt * P, (tt + 1) * P)
                done = three(four[tt][0][:], h_hi[:, k, cut], h_lo[:, k, cut], w_h, w_l, k == 0, k == KT - 1,
                             token, four[tt][1] if k == 0 else None, h_ready[k])
            if last:
                close_slab(i, done)
        for tt in range(TT):
            v_ready = act.put(lambda e, bank=four[tt][0], tt=tt, half=half: e.copy(v_nat[:, tt, half * S:(half + 1) * S], bank[:]), done, old)
            give(four[tt][0], v_ready)

    qk_ready = [None] * 16
    qk_projected = [None]

    def project_queries_keys():
        for pair in QK_PAIRS:
            for n in pair:
                for bank, token in project_steps(h_hi, h_lo, range(KT), h_ready):
                    yield
                qk_ready[n] = act.put(lambda e: e.copy(qk_t[:, n, :], bank[:]), token, old)
                give(bank, qk_ready[n])
        qk_projected[0] = token

    maps = [(c, 4 + c, DH * m, 2 * c + m) for c in range(DIFF_HEADS) for m in range(2)]
    maps += [(8 + h // 2, 12 + h // 2, DH * (h % 2), 8 + h) for h in range(DIL_HEADS)]
    probs = sb("probs", [P, UNITS_AHEAD, 2, S], stack=att)
    prob_t = sb("prob_t", [P, 2, TT, S], stack=att)
    probs_reader = [None] * UNITS_AHEAD
    prob_t_reader = [None] * 2
    b_ready = [None] * KT

    def scores(unit):
        slot, width = unit["n"] % UNITS_AHEAD, (unit["qt"] + 1) * P
        unit["maps_done"] = []
        for m, mid in enumerate(unit["maps"]):
            qi, ki, off, bc = maps[mid]
            rows, cols_q = slice(off, off + DH), slice(width - P, width)
            bank, reader = take()
            a = pe.put(lambda e: e.matmul(bank[:, 0:width], qk_t[rows, qi, cols_q], qk_t[rows, ki, 0:width], start=True, stop=True),
                       qk_ready[qi], qk_ready[ki], reader)
            w = probs[:, slot, m, 0:width]
            k = 2 * (mid * TT + unit["qt"])
            top_c, sum_c = stat[:, k:k + 1], stat[:, k + 1:k + 2]
            a = dve.put(lambda e: e.tensor_tensor_reduce(out=w, in0=bank[:, 0:width], in1=bias[:, bc % 4, S - width:S], scale=DH ** -0.5,
                                                         scalar=-3.0e38, op0=ALU.add, op1=ALU.max, accum_out=top_c),
                        a, bias_ready[bc], probs_reader[slot], old)
            give(bank, a)
            bias_reader[bc % 4] = a
            if unit["qt"] == TT - 1:
                load_bias(bc + 4)
            b = dve.put(lambda e: e.tensor_scalar(top_c, top_c, -1.0, None, ALU.mult), a)
            if unit["diff"]:
                b = act.put(lambda e: e.activation(w, w, ACT.Exp, bias=top_c, accum_out=sum_c), b)
            else:
                b = act.put(lambda e: e.activation(w, w, ACT.Exp, bias=top_c), b)
            unit["maps_done"].append((w, sum_c, b))

    def weights(unit):
        width = (unit["qt"] + 1) * P
        done = []
        for m, (w, sum_c, b) in enumerate(unit["maps_done"]):
            if not unit["diff"]:
                b = dve.put(lambda e: e.tensor_tensor_reduce(out=w, in0=w, in1=mult[:, S - width:S], scale=1.0, scalar=0.0,
                                                             op0=ALU.mult, op1=ALU.add, accum_out=sum_c), b, att_ready)
            b = dve.put(lambda e: e.reciprocal(sum_c, sum_c), b)
            done.append((w, sum_c, b))
        w0, s0, b0 = done[0]
        if unit["diff"]:
            w1, s1, b1 = done[1]
            b1 = dve.put(lambda e: e.tensor_tensor(s1, s1, lam[:, 5:6], ALU.mult), b1, lam_ready)
            b0 = dve.put(lambda e: e.tensor_scalar(w0, w0, s0, None, ALU.mult), b0)
            unit["w"] = dve.put(lambda e: e.scalar_tensor_tensor(w0, w1, s1, w0, ALU.mult, ALU.subtract, reverse1=True), b1, b0)
        else:
            unit["w"] = dve.put(lambda e: e.tensor_scalar(w0, w0, s0, None, ALU.mult), b0)

    def turn(unit):
        slot, qt = unit["n"] % UNITS_AHEAD, unit["qt"]
        bank, reader = take()
        for kt in range(qt + 1):
            a = pe.put(lambda e: e.transpose(bank[:, kt * P:(kt + 1) * P], probs[:, slot, 0, kt * P:(kt + 1) * P], ident[:]),
                       unit["w"], reader)
        probs_reader[slot] = a
        k = unit["head"] % 2
        a = act.put(lambda e: e.copy(prob_t[:, k, 0:qt + 1, qt * P:(qt + 1) * P],
                                     bank[:, 0:(qt + 1) * P].rearrange("p (k q) -> p k q", q=P)), a, prob_t_reader[k], old)
        give(bank, a)
        return a

    pair_bank = {}

    def weigh_values(unit, ready_t):
        head, k = unit["head"], unit["head"] % 2
        if unit["diff"]:
            bank, reader = take()
            rows, v_cols = slice(0, P), slice(head * P, (head + 1) * P)
        else:
            h = head - DIFF_HEADS
            if h % 2 == 0:
                pair_bank["bank"] = take()
            bank, reader = pair_bank["bank"]
            rows, v_cols = slice(DH * (h % 2), DH * (h % 2 + 1)), slice(S + h * DH, S + (h + 1) * DH)
        for kt in range(TT):
            a = pe.put(lambda e: e.matmul(bank[rows, kt * P:], v_nat[:, kt, v_cols], prob_t[:, k, kt, kt * P:], start=kt == 0, stop=kt == TT - 1),
                       ready_t, v_ready, reader)
        prob_t_reader[k] = a
        if unit["diff"]:
            oa_ready.append(act.put(lambda e: e.copy(qk_t[:, head, :], bank[:]), a))
            give(bank, oa_ready[-1])
        elif h % 2:
            a = act.put(lambda e: e.copy(qk_t[:, 8 + h // 2, :], bank[:]), a)
            give(bank, a)
            finished.append((DIFF_HEADS + h // 2, qk_t[:, 8 + h // 2, :], a))

    oa_ready, finished = [], []

    def split_finished(lo_on):
        if finished and qk_projected[0]:
            c, out, token = finished.pop(0)
            b_ready[c] = split(out, h_hi[:, c, :], h_lo[:, c, :], token, qk_projected[0], lo_on=lo_on)

    def diff_norm():
        for c in range(DIFF_HEADS):
            i, square, r = scratch()
            a = act.put(lambda e: e.activation(square, qk_t[:, c, :], ACT.Square), oa_ready[c], r)
            yield
            bank, reader = take()
            token = tmp_reader[i] = pe.put(lambda e: e.matmul(bank[:], ones[:], square, start=True, stop=True), a, reader)
            yield
            a = dve.put(lambda e: e.tensor_scalar(qk_t[:, DIFF_HEADS + c, :], bank[:], 1.0 / P, EPS, ALU.mult, ALU.add), token)
            give(bank, a)
        a = act.put(lambda e: e.activation(qk_t[:, DIFF_HEADS:2 * DIFF_HEADS, :], qk_t[:, DIFF_HEADS:2 * DIFF_HEADS, :], ACT.Sqrt), a)
        yield
        yield
        for c in range(DIFF_HEADS):
            b = dve.put(lambda e: e.reciprocal(qk_t[:, DIFF_HEADS + c, :], qk_t[:, DIFF_HEADS + c, :]), a)
            yield
            b = dve.put(lambda e: e.scalar_tensor_tensor(qk_t[:, c, :], qk_t[:, c, :], subln[:, 0:1], qk_t[:, DIFF_HEADS + c, :],
                                                         ALU.mult, ALU.mult), b, lam_ready)
            finished.append((c, qk_t[:, c, :], b))
            yield

    units = [{"head": head, "qt": qt, "diff": head < DIFF_HEADS,
              "maps": [2 * head, 2 * head + 1] if head < DIFF_HEADS else [DIFF_HEADS + head]}
             for head in range(DIFF_HEADS + DIL_HEADS) for qt in range(TT)]
    norm_work, qk_work = diff_norm(), project_queries_keys()
    blocks_done = 0

    def project_until(blocks):
        nonlocal blocks_done
        while blocks_done < blocks:
            next(qk_work, None)
            blocks_done += 1

    last_block = len(QK_PAIRS) * 2 * KT + 1
    turned = []
    for n in range(len(units) + UNITS_AHEAD):
        if n >= UNITS_AHEAD:
            if turned:
                weigh_values(*turned.pop())
            unit = units[n - UNITS_AHEAD]
            ready_t = turn(unit)
            if unit["qt"] == TT - 1:
                turned.append((unit, ready_t))
            split_finished(pool)
            if unit["head"] > DIFF_HEADS:
                next(norm_work, None)
        if n < len(units):
            units[n]["n"] = n
            head, qt = units[n]["head"], units[n]["qt"]
            pair, share = (head, qt / TT) if head < DIFF_HEADS else divmod(head + DIFF_HEADS + qt / TT, 2)
            if head >= DIFF_HEADS:
                pair, share = int(pair), share / 2
            project_until(min(last_block, int((pair + 1 + share) * 2 * KT) + 1))
            scores(units[n])
        if 1 <= n <= len(units):
            weights(units[n - 1])
    weigh_values(*turned.pop())
    finish(norm_work)
    while finished:
        split_finished(dve)

    pair = project_both(h_hi, h_lo, b_ready)
    for n in range(KT):
        bank, token = pair[n] if n < 2 else project(h_hi, h_lo, range(KT), b_ready)
        a = dve.put(lambda e, bank=bank, n=n: e.tensor_tensor(x[:, n, :], bank[:], x[:, n, :], ALU.add), token)
        give(bank, a)
        x_tok[n] = a
        add_square(n)
    h_ready = [scaled(k, col("ffn2_norm_2", k), token) for k in range(KT)]
    att_done = [token, (act, act.count), (dve, dve.count), (pool, pool.count)]
    att.close()

    swiglu("ffn2", att_done, h_ready, rstd, one_root())
    norm_in_place("final_norm_2", norm_root())
    out_done = counter("out_done")
    for k in range(KT):
        stored = sp.dma(t["out"][:, k, :], x[:, k, :], out_done, x_tok[k])
    sp.wait(stored)
    sp.wait(g_written)
    sp.wait((bias_out, bias_out.count))
    assert used[0] == len(split_slabs)
    nc.all_engine_barrier()


def slabs(w):
    k, n = w.shape
    b = w.reshape(k // P, P, n // P, P).transpose(2, 0, 1, 3).reshape(-1, SLAB, P, P)
    return np.ascontiguousarray(b.transpose(0, 2, 1, 3).reshape(-1, P, SLAB * P))


def wide_slabs(w):
    b = w.reshape(w.shape[0] // (2 * P), 2, P, w.shape[1])
    return np.ascontiguousarray(b.transpose(0, 2, 1, 3).reshape(-1, P, SLAB * P))


def columns(v):
    return v.reshape(-1, P).T


def bucket_of(dist):
    n = np.maximum(dist, 0)
    nf = np.maximum(n, 1).astype(np.float32)
    large = 16 + (np.log(nf / 16) / math.log(2048 / 16) * 16).astype(np.int32)
    return np.where(n < 16, n, np.minimum(large, 31))


def windows_of(dist):
    n = sum(((dist >= 0) & (dist % r == 0) & (dist <= w)).astype(np.int32) for w, r in ((128, 1), (512, 4), (2048, 16)))
    return n


def constants():
    i = np.arange(P, dtype=np.float32)
    fix = np.ones((P, CT, PAD_POOL), np.float32)
    for c, w in enumerate(POOL_WINDOWS):
        fix[:, c, :] = w / np.minimum(np.arange(1, PAD_POOL + 1), w)
    dist = S - 1 - np.arange(BIAS_L)
    buckets = np.zeros((DH, 2, BIAS_L), np.float32)
    for kind in range(2):
        buckets[bucket_of(dist), kind, np.arange(BIAS_L)] = 1.0
        buckets[32, kind, :] = (dist < 0) if kind == 0 else (windows_of(dist) == 0)
    z = np.arange(P)[:, None] + (S - P) - np.arange(S)[None, :]
    return {
        "ident": np.eye(P, dtype=np.float32),
        "ones": np.ones((P, P), np.float32),
        "iota128": np.ascontiguousarray(np.broadcast_to(i, (P, P))),
        "iota16": np.ascontiguousarray(np.broadcast_to(i[:TOPK], (P, TOPK))),
        "window_fix": fix,
        "buckets": buckets,
        "mult": windows_of(z).astype(np.float32),
    }


def laid_out(a):
    o = dict(constants())
    o["x"] = np.ascontiguousarray(a["x"][0].T.reshape(KT, P, S).transpose(1, 0, 2))
    vectors = {n: columns(a[n].reshape(-1)) for n in COLS if n != "dw_kernel"}
    vectors["dw_kernel"] = a["dw_kernel"][0].T.reshape(CT, P, CONV_K).transpose(1, 0, 2).reshape(P, -1)
    o["cols"] = np.ascontiguousarray(np.concatenate([vectors[n] for n in COLS], axis=1))
    ada = a["ada_w"][0].reshape(KT, P, 6, D)
    o["ada_w"] = np.ascontiguousarray(ada.transpose(2, 0, 1, 3).reshape(6 * KT, P, D))
    w = a["w_in"][0]
    value_gate = [w[:, CW + half * CW + c * P:CW + half * CW + (c + 1) * P] for c in range(CT) for half in range(2)]
    o["w_in"] = slabs(np.concatenate([w[:, :CW]] + value_gate + [w[:, 3 * CW:]], axis=1))
    o["pool_w"] = np.ascontiguousarray(a["pool_w"][0].transpose(1, 0, 2))
    o["w_merge"] = slabs(np.concatenate([a["pool_up"][0], a["conv_out"][0]], axis=0))
    o["w_out"] = slabs(a["w_out"][0])
    o["w_query"] = slabs(a["w_query"][0])
    o["keys"] = np.ascontiguousarray(np.stack([a["sub_keys_1"][0].T, a["sub_keys_2"][0].T], axis=1))
    u = a["expert_u"][0].reshape(EXPERT_TILES, P, KT, P)
    o["expert_u"] = np.ascontiguousarray(u.transpose(0, 3, 2, 1).reshape(EXPERT_TILES, P, KT * P))
    v = a["expert_v"][0].reshape(N_GROUPS, GROUP, P, KT, P)
    o["expert_v"] = np.ascontiguousarray(v.transpose(0, 3, 2, 1, 4).reshape(N_GROUPS * KT, P, GROUP * P))
    for n in ("ffn1", "ffn2"):
        g = a[f"{n}_w_gate_2"][0].reshape(D, FT, P)
        up = a[f"{n}_w_up_2"][0].reshape(D, FT, P)
        o[f"{n}_gate_up"] = slabs(np.stack([g, up], axis=2).reshape(D, 2 * D_FF))
        o[f"{n}_down"] = slabs(a[f"{n}_w_down_2"][0])
    w = a["w_in_2"][0]
    qa, ka, va, qb, kb, vb = (w[:, i * CW:(i + 1) * CW] for i in range(6))
    o["w_in_2"] = np.concatenate([slabs(np.concatenate([qa, ka, qb, kb], axis=1)), wide_slabs(va), wide_slabs(vb)])
    o["w_out_2"] = slabs(a["w_out_2"][0])
    lam = np.stack([a["lambda_q1_2"][0], a["lambda_q2_2"][0], a["lambda_k1_2"][0], a["lambda_k2_2"][0]])
    o["lam_in"] = np.ascontiguousarray(np.broadcast_to(lam, (P, 4, DH)))
    table = np.zeros((DH, N_MAPS), np.float32)
    table[:32] = a["rel_bias_2"]
    table[32] = NEG
    o["rel_bias"] = table
    return o


def kernel(**inputs):
    import concourse.bacc as bacc
    from concourse.bass_utils import run_bass_kernel_spmd

    arrays = laid_out({n: np.asarray(v) for n, v in inputs.items()})
    nc = bacc.Bacc("TRN2", target_bir_lowering=False, num_devices=1)
    t = {n: nc.dram_tensor(n + "_dram", v.shape, F32, kind="ExternalInput").ap() for n, v in arrays.items()}
    t["out"] = nc.dram_tensor("out_dram", (P, KT, S), F32, kind="ExternalOutput").ap()
    t["g_scratch"] = nc.dram_tensor("g_scratch", (S // CHUNK, P, EXPERT_TILES, CHUNK), F32, kind="Internal").ap()
    t["bias_scratch"] = nc.dram_tensor("bias_scratch", (P, N_MAPS, BIAS_L), F32, kind="Internal").ap()
    build(nc, t)
    r = run_bass_kernel_spmd(nc, [{n + "_dram": v for n, v in arrays.items()}], core_ids=[0])
    out = r.results[0]["out_dram"]
    return np.ascontiguousarray(out.transpose(2, 1, 0).reshape(1, S, D))
```
